# Optimizing a Trainium2 kernel written in Bass

```python
import jax, jax.numpy as jnp
from jax import lax
import numpy as np
import math

D_MODEL = 1024
BATCH = 1
SEQ = 512
DEPTH = 1

MLSTM_HEADS = 4
MLSTM_HEAD_DIM = D_MODEL // 8
MLSTM_WIDTH = MLSTM_HEADS * MLSTM_HEAD_DIM
HGRN_HEADS = 4
HGRN_HEAD_DIM = D_MODEL // 8
HGRN_WIDTH = HGRN_HEADS * HGRN_HEAD_DIM
MIX_WIDTH = MLSTM_WIDTH + HGRN_WIDTH
CONV_WIDTH = 4
MLSTM_CHUNK = 64
HGRN_CHUNK = 16
D_FF = ((8 * D_MODEL // 3 + 255) // 256) * 256
FFN_RESIDUAL_WEIGHT = 0.5
EPS = 1e-6
N_MOD = 9
M_NEG = -1e30
PROJ_SPLITS = [MLSTM_WIDTH, MLSTM_WIDTH, MLSTM_WIDTH, MLSTM_WIDTH, 2 * MLSTM_HEADS,
               HGRN_WIDTH, HGRN_WIDTH, HGRN_WIDTH, HGRN_WIDTH]
PROJ_WIDTH = sum(PROJ_SPLITS)
PROJ_IDX = list(np.cumsum(PROJ_SPLITS)[:-1])


def rmsnorm(x, g):
    xf = x.astype(jnp.float32)
    y = xf * lax.rsqrt(jnp.mean(xf * xf, axis=-1, keepdims=True) + EPS)
    return (y * g.astype(jnp.float32)).astype(x.dtype)

def head_rmsnorm(h, g, n_heads):
    B, S, W = h.shape
    hf = h.astype(jnp.float32).reshape(B, S, n_heads, W // n_heads)
    hf = hf * lax.rsqrt(jnp.mean(hf * hf, axis=-1, keepdims=True) + EPS)
    return hf.reshape(B, S, W) * g.astype(jnp.float32)

def split_heads(a, n_heads):
    B, S, W = a.shape
    return a.reshape(B, S, n_heads, W // n_heads).transpose(0, 2, 1, 3)

def merge_heads(a):
    B, H, S, dh = a.shape
    return a.transpose(0, 2, 1, 3).reshape(B, S, H * dh)

def to_chunks(a, L):
    B, H, S = a.shape[:3]
    return jnp.moveaxis(a.reshape(B, H, S // L, L, *a.shape[3:]), 2, 0)

def from_chunks(a):
    nc, B, H, L, d = a.shape
    return jnp.moveaxis(a, 0, 2).reshape(B, H, nc * L, d)

def causal_dwconv(x, w, b):
    C = x.shape[-1]
    y = lax.conv_general_dilated(x, w.astype(x.dtype)[:, None, :], window_strides=(1,),
                                 padding=[(CONV_WIDTH - 1, 0)],
                                 dimension_numbers=('NWC', 'WIO', 'NWC'),
                                 feature_group_count=C)
    return y + b.astype(x.dtype)

def mlstm_chunkwise(q, k, v, log_i, log_f):
    B, H, S, dh = q.shape
    L = MLSTM_CHUNK
    causal = jnp.tril(jnp.ones((L, L), dtype=bool))
    xs = (to_chunks(q, L), to_chunks(k, L), to_chunks(v, L), to_chunks(log_i, L), to_chunks(log_f, L))

    def step(carry, inp):
        C, n, m = carry
        qb, kb, vb, li, lf = inp
        bcum = jnp.cumsum(lf, axis=-1)
        d = bcum[..., :, None] - bcum[..., None, :] + li[..., None, :]
        d = jnp.where(causal, d, -jnp.inf)
        inter = bcum + m[..., None]
        m_t = jnp.maximum(inter, jnp.max(d, axis=-1))
        w = jnp.exp(d - m_t[..., None])
        a = jnp.exp(inter - m_t)
        s = jnp.einsum('bhtd,bhsd->bhts', qb, kb) * w
        num = a[..., None] * jnp.einsum('bhtd,bhde->bhte', qb, C) + jnp.einsum('bhts,bhse->bhte', s, vb)
        den = a * jnp.einsum('bhtd,bhd->bht', qb, n) + jnp.sum(s, axis=-1)
        h = num / jnp.maximum(jnp.abs(den), jnp.exp(-m_t))[..., None]
        m_new = m_t[..., -1]
        g = jnp.exp(bcum[..., -1:] - bcum + li - m_new[..., None])
        decay = jnp.exp(bcum[..., -1] + m - m_new)
        C_new = decay[..., None, None] * C + jnp.einsum('bhs,bhsd,bhse->bhde', g, kb, vb)
        n_new = decay[..., None] * n + jnp.einsum('bhs,bhsd->bhd', g, kb)
        return (C_new, n_new, m_new), h

    init = (jnp.zeros((B, H, dh, dh), jnp.float32), jnp.zeros((B, H, dh), jnp.float32),
            jnp.full((B, H), M_NEG, jnp.float32))
    _, hs = lax.scan(step, init, xs)
    return from_chunks(hs)

def hgrn2_chunkwise(q, k, v, log_f):
    B, H, S, dk = q.shape
    dv = v.shape[-1]
    L = HGRN_CHUNK
    causal = jnp.tril(jnp.ones((L, L), dtype=bool))[:, :, None]
    xs = (to_chunks(q, L), to_chunks(k, L), to_chunks(v, L), to_chunks(log_f, L))

    def step(Sst, inp):
        qb, kb, vb, gb = inp
        bc = jnp.cumsum(gb, axis=2)
        inter = jnp.einsum('bhtc,bhce->bhte', qb * jnp.exp(bc), Sst)
        dec = jnp.exp(jnp.where(causal, bc[:, :, :, None, :] - bc[:, :, None, :, :], -jnp.inf))
        att = jnp.einsum('bhtc,bhsc,bhtsc->bhts', qb, kb, dec)
        o = inter + jnp.einsum('bhts,bhse->bhte', att, vb)
        S_new = jnp.exp(bc[:, :, -1])[..., None] * Sst + jnp.einsum(
            'bhsc,bhse->bhce', kb * jnp.exp(bc[:, :, -1:] - bc), vb)
        return S_new, o

    _, os = lax.scan(step, jnp.zeros((B, H, dk, dv), jnp.float32), xs)
    return from_chunks(os)

def swiglu(y, w_gate, w_up, w_down):
    return (jax.nn.silu(y @ w_gate) * (y @ w_up)) @ w_down

def token_mix(y, w_in, conv_w, conv_b, gate_b, mnorm_g, lb, hnorm_g, w_out):
    f32 = jnp.float32
    p = y @ w_in
    mq, mk, mv, mo, mif, hq, hf, hi, hg = jnp.split(p, PROJ_IDX, axis=-1)

    qk = jax.nn.silu(causal_dwconv(jnp.concatenate([mq, mk], axis=-1), conv_w, conv_b))
    mq, mk = jnp.split(qk, 2, axis=-1)
    q = split_heads(mq, MLSTM_HEADS).astype(f32)
    k = split_heads(mk, MLSTM_HEADS).astype(f32) * (MLSTM_HEAD_DIM ** -0.5)
    v = split_heads(mv, MLSTM_HEADS).astype(f32)
    gates = (mif.astype(f32) + gate_b.astype(f32)).transpose(0, 2, 1)
    log_i = gates[:, :MLSTM_HEADS]
    log_f = jax.nn.log_sigmoid(gates[:, MLSTM_HEADS:])
    hm = merge_heads(mlstm_chunkwise(q, k, v, log_i, log_f))
    out_m = head_rmsnorm(hm, mnorm_g, MLSTM_HEADS) * jax.nn.sigmoid(mo.astype(f32))

    fgate = lb.astype(f32) + (1.0 - lb.astype(f32)) * jax.nn.sigmoid(hf.astype(f32))
    hq_ = split_heads(jax.nn.silu(hq.astype(f32)), HGRN_HEADS)
    hk_ = split_heads(1.0 - fgate, HGRN_HEADS)
    hv_ = split_heads(hi.astype(f32), HGRN_HEADS)
    hlf = split_heads(jnp.log(fgate), HGRN_HEADS)
    ho = merge_heads(hgrn2_chunkwise(hq_, hk_, hv_, hlf))
    out_h = head_rmsnorm(ho, hnorm_g, HGRN_HEADS) * jax.nn.silu(hg.astype(f32))

    merged = jnp.concatenate([out_m, out_h], axis=-1).astype(y.dtype)
    return merged @ w_out

def first_inputs(seed: int = 0) -> dict:
    key = jax.random.key(seed)
    ks = jax.random.split(key, 32)
    nrm = jax.random.normal
    D, F = D_MODEL, D_FF

    def gain(k, n):
        return 1.0 + 0.05 * nrm(k, (DEPTH, n), jnp.float32)

    forget_bias = jnp.linspace(3.0, 6.0, MLSTM_HEADS, dtype=jnp.float32)[None, :] \
        + 0.1 * nrm(ks[14], (DEPTH, MLSTM_HEADS), jnp.float32)
    input_bias = 0.1 * nrm(ks[15], (DEPTH, MLSTM_HEADS), jnp.float32)
    return {
        "x": nrm(ks[0], (BATCH, SEQ, D), jnp.float32),
        "c": nrm(ks[1], (BATCH, D), jnp.float32),
        "ada_w": 0.5 * (D ** -0.5) * nrm(ks[2], (DEPTH, D, N_MOD * D), jnp.float32),
        "ada_b": 0.02 * nrm(ks[3], (DEPTH, N_MOD * D), jnp.float32),
        "ffn1_pre_g": gain(ks[4], D),
        "ffn1_post_g": gain(ks[5], D),
        "ffn1_w_gate": (D ** -0.5) * nrm(ks[6], (DEPTH, D, F), jnp.float32),
        "ffn1_w_up": (D ** -0.5) * nrm(ks[7], (DEPTH, D, F), jnp.float32),
        "ffn1_w_down": (F ** -0.5) * nrm(ks[8], (DEPTH, F, D), jnp.float32),
        "mix_pre_g": gain(ks[9], D),
        "mix_post_g": gain(ks[10], D),
        "w_in": (D ** -0.5) * nrm(ks[11], (DEPTH, D, PROJ_WIDTH), jnp.float32),
        "mlstm_conv_w": (CONV_WIDTH ** -0.5) * nrm(ks[12], (DEPTH, CONV_WIDTH, 2 * MLSTM_WIDTH), jnp.float32),
        "mlstm_conv_b": 0.02 * nrm(ks[13], (DEPTH, 2 * MLSTM_WIDTH), jnp.float32),
        "mlstm_gate_b": jnp.concatenate([input_bias, forget_bias], axis=-1),
        "mlstm_norm_g": gain(ks[16], MLSTM_WIDTH),
        "hgrn_lb_logits": nrm(ks[17], (DEPTH + 1, HGRN_WIDTH), jnp.float32),
        "hgrn_norm_g": gain(ks[18], HGRN_WIDTH),
        "w_out": (MIX_WIDTH ** -0.5) * nrm(ks[19], (DEPTH, MIX_WIDTH, D), jnp.float32),
        "ffn2_pre_g": gain(ks[20], D),
        "ffn2_post_g": gain(ks[21], D),
        "ffn2_w_gate": (D ** -0.5) * nrm(ks[22], (DEPTH, D, F), jnp.float32),
        "ffn2_w_up": (D ** -0.5) * nrm(ks[23], (DEPTH, D, F), jnp.float32),
        "ffn2_w_down": (F ** -0.5) * nrm(ks[24], (DEPTH, F, D), jnp.float32),
    }

def first_block(x, c, ada_w, ada_b, ffn1_pre_g, ffn1_post_g, ffn1_w_gate, ffn1_w_up, ffn1_w_down,
              mix_pre_g, mix_post_g, w_in, mlstm_conv_w, mlstm_conv_b, mlstm_gate_b, mlstm_norm_g,
              hgrn_lb_logits, hgrn_norm_g, w_out, ffn2_pre_g, ffn2_post_g, ffn2_w_gate, ffn2_w_up,
              ffn2_w_down):
    lb_all = jnp.cumsum(jax.nn.softmax(hgrn_lb_logits.astype(jnp.float32), axis=0), axis=0)
    sc = jax.nn.silu(c)
    h = x
    for l in range(DEPTH):
        mod = (sc @ ada_w[l] + ada_b[l])[:, None, :]
        (sh1, sc1, g1, sh2, sc2, g2, sh3, sc3, g3) = jnp.split(mod, N_MOD, axis=-1)

        y = rmsnorm(h, ffn1_pre_g[l]) * (1.0 + sc1) + sh1
        y = swiglu(y, ffn1_w_gate[l], ffn1_w_up[l], ffn1_w_down[l])
        h = h + FFN_RESIDUAL_WEIGHT * g1 * rmsnorm(y, ffn1_post_g[l])

        y = rmsnorm(h, mix_pre_g[l]) * (1.0 + sc2) + sh2
        y = token_mix(y, w_in[l], mlstm_conv_w[l], mlstm_conv_b[l], mlstm_gate_b[l], mlstm_norm_g[l],
                      lb_all[l], hgrn_norm_g[l], w_out[l])
        h = h + g2 * rmsnorm(y, mix_post_g[l])

        y = rmsnorm(h, ffn2_pre_g[l]) * (1.0 + sc3) + sh3
        y = swiglu(y, ffn2_w_gate[l], ffn2_w_up[l], ffn2_w_down[l])
        h = h + FFN_RESIDUAL_WEIGHT * g3 * rmsnorm(y, ffn2_post_g[l])
    return h


DEPTH_2 = 2

N_MIXERS = 2
D_FF_2 = 4 * D_MODEL
NORM_EPS = 1e-6
GLA_HEADS = 4
GLA_DK = D_MODEL // 2 // GLA_HEADS
GLA_DV = D_MODEL // GLA_HEADS
GLA_GATE_RANK = 16
GLA_TAU = 16.0
GLA_CHUNK = 64
GLA_IN = 2 * GLA_HEADS * GLA_DK + 2 * D_MODEL + GLA_GATE_RANK
DIFF_HEADS = 8
DIFF_DH = D_MODEL // DIFF_HEADS // 2
DIFF_DV = 2 * DIFF_DH
DIFF_IN = 3 * D_MODEL
ROPE_THETA = 500000.0
ROPE_DIM = DIFF_DH // 4
Q_BLOCK = 128
N_GLA = (DEPTH_2 + 1) // 2
N_DIFF = DEPTH_2 // 2


def rmsnorm_2(x, g):
    xf = x.astype(jnp.float32)
    y = xf * lax.rsqrt(jnp.mean(xf * xf, axis=-1, keepdims=True) + NORM_EPS)
    return (y * g.astype(jnp.float32)).astype(x.dtype)

def rope_partial(x, cos, sin):
    half = ROPE_DIM // 2
    cos = cos.astype(x.dtype)
    sin = sin.astype(x.dtype)
    x1 = x[..., :half]
    x2 = x[..., half:ROPE_DIM]
    rest = x[..., ROPE_DIM:]
    return jnp.concatenate([x1 * cos - x2 * sin, x2 * cos + x1 * sin, rest], axis=-1)

def gla_mixer(h, w_in, w_a2, b_a, b_r, norm_g, w_o):
    B, T, _ = h.shape
    H, dk, dv, C = GLA_HEADS, GLA_DK, GLA_DV, GLA_CHUNK
    n = T // C
    hk = H * dk
    f32 = jnp.float32
    q, k, v, r, a_lr = jnp.split(h @ w_in, [hk, 2 * hk, 2 * hk + D_MODEL, 2 * hk + 2 * D_MODEL], axis=-1)
    log_a = jax.nn.log_sigmoid((a_lr @ w_a2 + b_a).astype(f32)) / GLA_TAU

    def chunks(t, d):
        return t.reshape(B, n, C, H, d)

    q = chunks(q.astype(f32), dk) * (dk ** -0.5)
    k = chunks(k.astype(f32), dk)
    v = chunks(v.astype(f32), dv)
    b = jnp.cumsum(chunks(log_a, dk), axis=2)
    b_last = b[:, :, -1:]
    q_dec = q * jnp.exp(b)
    k_intra = k * jnp.exp(-b)
    k_state = k * jnp.exp(b_last - b)

    causal = jnp.tril(jnp.ones((C, C), dtype=bool))
    scores = jnp.einsum('bnchk,bnshk->bnhcs', q_dec, k_intra)
    scores = jnp.where(causal, scores, 0.0)
    o_intra = jnp.einsum('bnhcs,bnshv->bnchv', scores, v)

    def step(state, inp):
        q_c, k_c, v_c, decay = inp
        o_c = jnp.einsum('bchk,bhkv->bchv', q_c, state)
        state = state * jnp.exp(decay)[..., None] + jnp.einsum('bchk,bchv->bhkv', k_c, v_c)
        return state, o_c

    xs = (jnp.moveaxis(q_dec, 1, 0), jnp.moveaxis(k_state, 1, 0),
          jnp.moveaxis(v, 1, 0), jnp.moveaxis(b_last[:, :, 0], 1, 0))
    s0 = jnp.zeros((B, H, dk, dv), f32)
    _, o_inter = lax.scan(step, s0, xs)
    o = o_intra + jnp.moveaxis(o_inter, 0, 1)
    o = rmsnorm_2(o, norm_g).reshape(B, T, D_MODEL)
    o = o * jax.nn.silu((r + b_r).astype(f32))
    return o.astype(h.dtype) @ w_o

def diff_mixer(h, cos, sin, w_in, lam_vecs, subln_g, w_o, lambda_init):
    B, T, _ = h.shape
    H, dh, dv = DIFF_HEADS, DIFF_DH, DIFF_DV
    f32 = jnp.float32
    q, k, v = jnp.split(h @ w_in, 3, axis=-1)
    q = rope_partial(q.reshape(B, T, H, 2, dh), cos, sin) * (dh ** -0.5)
    k = rope_partial(k.reshape(B, T, H, 2, dh), cos, sin)
    q = q.transpose(0, 2, 3, 1, 4)
    k = k.transpose(0, 2, 3, 1, 4)
    v = v.reshape(B, T, H, dv).transpose(0, 2, 1, 3)
    lf = lam_vecs.astype(f32)
    lam = jnp.exp(jnp.sum(lf[0] * lf[1])) - jnp.exp(jnp.sum(lf[2] * lf[3])) + lambda_init
    outs = []
    for i in range(T // Q_BLOCK):
        L = (i + 1) * Q_BLOCK
        qb = q[:, :, :, i * Q_BLOCK:L]
        s = jnp.einsum('bhiqd,bhikd->bhiqk', qb, k[:, :, :, :L]).astype(f32)
        q_idx = i * Q_BLOCK + jnp.arange(Q_BLOCK)
        mask = jnp.arange(L)[None, :] <= q_idx[:, None]
        p = jax.nn.softmax(jnp.where(mask, s, -jnp.inf), axis=-1)
        a = p[:, :, 0] - lam * p[:, :, 1]
        outs.append(jnp.einsum('bhqk,bhkv->bhqv', a.astype(v.dtype), v[:, :, :L]))
    o = jnp.concatenate(outs, axis=2)
    o = rmsnorm_2(o, subln_g) * (1.0 - lambda_init)
    o = o.transpose(0, 2, 1, 3).reshape(B, T, D_MODEL)
    return o @ w_o

def second_inputs(seed: int = 0) -> dict:
    key = jax.random.key(seed)
    ks = jax.random.split(key, 24)
    D = D_MODEL
    nrm = jax.random.normal
    x = nrm(ks[0], (BATCH, SEQ, D), jnp.float32)
    c = nrm(ks[1], (BATCH, D), jnp.float32)
    offsets = jax.random.randint(ks[2], (BATCH, 1), 0, 4096, dtype=jnp.int32)
    positions = (offsets + jnp.arange(SEQ, dtype=jnp.int32)[None, :]).astype(jnp.int32)
    return {
        "x": x,
        "c": c,
        "positions": positions,
        "ada_w": nrm(ks[3], (DEPTH_2, D, 6 * D), jnp.float32) * (0.5 * D ** -0.5),
        "ada_b": nrm(ks[4], (DEPTH_2, 6 * D), jnp.float32) * 0.02,
        "norm_g": 1.0 + 0.05 * nrm(ks[5], (DEPTH_2, 2, D), jnp.float32),
        "mlp_w1": nrm(ks[6], (DEPTH_2, D, D_FF_2), jnp.float32) * D ** -0.5,
        "mlp_w2": nrm(ks[7], (DEPTH_2, D_FF_2, D), jnp.float32) * D_FF_2 ** -0.5,
        "gla_w_in": nrm(ks[8], (N_GLA, D, GLA_IN), jnp.float32) * D ** -0.5,
        "gla_w_a2": nrm(ks[9], (N_GLA, GLA_GATE_RANK, GLA_HEADS * GLA_DK), jnp.float32) * GLA_GATE_RANK ** -0.5,
        "gla_b_a": 0.5 + 0.1 * nrm(ks[10], (N_GLA, GLA_HEADS * GLA_DK), jnp.float32),
        "gla_b_r": 0.02 * nrm(ks[11], (N_GLA, D), jnp.float32),
        "gla_norm_g": 1.0 + 0.05 * nrm(ks[12], (N_GLA, GLA_DV), jnp.float32),
        "gla_w_o": nrm(ks[13], (N_GLA, D, D), jnp.float32) * D ** -0.5,
        "diff_w_in": nrm(ks[14], (N_DIFF, D, DIFF_IN), jnp.float32) * D ** -0.5,
        "diff_lambda": 0.1 * nrm(ks[15], (N_DIFF, 4, DIFF_DH), jnp.float32),
        "diff_subln_g": 1.0 + 0.05 * nrm(ks[16], (N_DIFF, DIFF_DV), jnp.float32),
        "diff_w_o": nrm(ks[17], (N_DIFF, D, D), jnp.float32) * D ** -0.5,
        "final_g": 1.0 + 0.05 * nrm(ks[18], (D,), jnp.float32),
    }

def second_block(x, c, positions, ada_w, ada_b, norm_g, mlp_w1, mlp_w2,
              gla_w_in, gla_w_a2, gla_b_a, gla_b_r, gla_norm_g, gla_w_o,
              diff_w_in, diff_lambda, diff_subln_g, diff_w_o, final_g):
    f32 = jnp.float32
    inv_freq = ROPE_THETA ** (-jnp.arange(0, ROPE_DIM, 2, dtype=f32) / ROPE_DIM)
    ang = positions.astype(f32)[..., None] * inv_freq
    cos = jnp.cos(ang)[:, :, None, None, :]
    sin = jnp.sin(ang)[:, :, None, None, :]
    c_act = jax.nn.silu(c)
    for i in range(DEPTH_2):
        mod = c_act @ ada_w[i] + ada_b[i]
        shift_t, scale_t, gate_t, shift_c, scale_c, gate_c = [
            m[:, None, :] for m in jnp.split(mod, 6, axis=-1)]
        h = rmsnorm_2(x, norm_g[i, 0]) * (1.0 + scale_t) + shift_t
        j = i // N_MIXERS
        if i % N_MIXERS == 0:
            y = gla_mixer(h, gla_w_in[j], gla_w_a2[j], gla_b_a[j], gla_b_r[j],
                          gla_norm_g[j], gla_w_o[j])
        else:
            lambda_init = 0.8 - 0.6 * math.exp(-0.3 * i)
            y = diff_mixer(h, cos, sin, diff_w_in[j], diff_lambda[j], diff_subln_g[j],
                           diff_w_o[j], lambda_init)
        x = x + gate_t * y
        h = rmsnorm_2(x, norm_g[i, 1]) * (1.0 + scale_c) + shift_c
        y = jnp.square(jax.nn.relu(h @ mlp_w1[i])) @ mlp_w2[i]
        x = x + gate_c * y
    return rmsnorm_2(x, final_g)


def setup_inputs(seed=0):
    out = dict(first_inputs(seed))
    for name, value in second_inputs(seed + 1).items():
        if name != "x":
            out[name + "_2"] = value
    return out


def reference(
    x, c, ada_w, ada_b, ffn1_pre_g, ffn1_post_g, ffn1_w_gate, ffn1_w_up, ffn1_w_down, mix_pre_g,
    mix_post_g, w_in, mlstm_conv_w, mlstm_conv_b, mlstm_gate_b, mlstm_norm_g, hgrn_lb_logits,
    hgrn_norm_g, w_out, ffn2_pre_g, ffn2_post_g, ffn2_w_gate, ffn2_w_up, ffn2_w_down, c_2,
    positions_2, ada_w_2, ada_b_2, norm_g_2, mlp_w1_2, mlp_w2_2, gla_w_in_2, gla_w_a2_2,
    gla_b_a_2, gla_b_r_2, gla_norm_g_2, gla_w_o_2, diff_w_in_2, diff_lambda_2, diff_subln_g_2,
    diff_w_o_2, final_g_2,
):
    x = first_block(
        x, c, ada_w, ada_b, ffn1_pre_g, ffn1_post_g, ffn1_w_gate, ffn1_w_up, ffn1_w_down,
        mix_pre_g, mix_post_g, w_in, mlstm_conv_w, mlstm_conv_b, mlstm_gate_b, mlstm_norm_g,
        hgrn_lb_logits, hgrn_norm_g, w_out, ffn2_pre_g, ffn2_post_g, ffn2_w_gate, ffn2_w_up,
        ffn2_w_down,
    )
    return second_block(
        x, c_2, positions_2, ada_w_2, ada_b_2, norm_g_2, mlp_w1_2, mlp_w2_2, gla_w_in_2,
        gla_w_a2_2, gla_b_a_2, gla_b_r_2, gla_norm_g_2, gla_w_o_2, diff_w_in_2, diff_lambda_2,
        diff_subln_g_2, diff_w_o_2, final_g_2,
    )


_drawn_inputs = setup_inputs


def setup_inputs(seed=0):
    import zlib

    import numpy as np

    out = dict(_drawn_inputs(seed))
    spreads = {}
    factors = {'ffn1_pre_g': 4.922,
     'ffn1_post_g': 6.568,
     'mix_pre_g': 2.886,
     'mix_post_g': 3.35,
     'mlstm_conv_b': 64.0,
     'mlstm_norm_g': 20.392,
     'hgrn_lb_logits': 2.69,
     'hgrn_norm_g': 4.793,
     'ffn2_pre_g': 5.425,
     'ffn2_post_g': 7.495,
     'gla_b_a_2': 4.99,
     'gla_b_r_2': 8.0,
     'gla_norm_g_2': 5.782,
     'diff_lambda_2': 2.817,
     'diff_subln_g_2': 6.263}
    for name, (base, spread) in spreads.items():
        noise = np.random.default_rng([zlib.crc32(name.encode()), seed]).standard_normal(out[name].shape)
        drawn = base * np.exp(spread * noise) if base else spread * noise
        out[name] = __import__('jax').numpy.asarray(drawn.astype(out[name].dtype))
    for name, factor in factors.items():
        out[name] = (out[name] * factor).astype(out[name].dtype)
    return out
```

```python
import math
from collections import deque
from contextlib import ExitStack

import numpy as np

import concourse.bass as bass
from concourse import mybir

S = 512
D = 1024
NT = D // 128
EPS = 1e-6
F1 = 2816
F2 = 4096
NRAW = 6
NW = 3
NTMP = 6
BIG = 1e30
LAMBDA_INIT = 0.8 - 0.6 * math.exp(-0.3)
MAGIC = 12582912.0
PI_A, PI_B, PI_C = 6.28125, 2029 / 2**20, 2 * math.pi - 6.28125 - 2029 / 2**20
INV_FREQ = np.power(np.float32(500000.0), -np.arange(0, 16, 2, dtype=np.float32) / np.float32(16)).astype(np.float32)

PARAMS = [
    ("c", 8), ("c_2", 8), ("ada_b", 72), ("ada_b_2", 96), ("ffn1_pre_g", 8), ("ffn1_post_g", 8),
    ("mix_pre_g", 8), ("mix_post_g", 8), ("mlstm_conv_w", 32), ("mlstm_conv_b", 8),
    ("mlstm_norm_g", 4), ("hgrn_lb_logits", 8), ("hgrn_norm_g", 4), ("ffn2_pre_g", 8),
    ("ffn2_post_g", 8), ("norm_g_2", 32), ("gla_b_a_2", 4), ("gla_b_r_2", 8), ("gla_norm_g_2", 2),
    ("diff_subln_g_2", 1), ("final_g_2", 8), ("mlstm_gate_b", 1), ("diff_lambda_2", 256),
]
IDENT, ONES, PERM, CAUS, CNEG, INVF_C, EPS_C, HPI_C, SEL_C, NCONST = 0, 128, 256, 384, 512, 640, 641, 642, 643, 647
LEVELS = [1, 2, 4, 8, 16, 32, 64]


def param_offsets():
    at, out = 0, {}
    for name, n in PARAMS:
        out[name] = at
        at += n
    return out, at


def constants():
    c = np.zeros((128, NCONST), np.float32)
    i = np.arange(128)
    c[:, IDENT:IDENT + 128] = np.eye(128)
    c[:, ONES:ONES + 128] = 1.0
    for g in (0, 64):
        for d in range(8):
            c[g + d + 8, PERM + g + d] = -1.0
            c[g + d, PERM + g + d + 8] = 1.0
            c[g + d, INVF_C] = c[g + d + 8, INVF_C] = INV_FREQ[d]
    c[:, CAUS:CAUS + 128] = np.where(i[None, :] < i[:, None], BIG, 0.0)
    c[:, CNEG:CNEG + 128] = np.where(i[None, :] > i[:, None], -BIG, 0.0)
    c[:, EPS_C] = EPS
    c[:, HPI_C] = math.pi / 2
    for h in range(4):
        c[4 + h, SEL_C + h] = 1.0
    m = np.zeros((128, 7, 128), np.float32)
    for n, h in enumerate(LEVELS):
        s, t = i[:, None], i[None, :]
        m[:, n, :] = (s // (2 * h) == t // (2 * h)) & (s % (2 * h) < h) & (t % (2 * h) >= h)
    return c, m.reshape(128, 896)


class Queue:

    def __init__(self, engine, sem):
        self.engine, self.sem, self.n, self.seen = engine, sem, 0, {}

    def wait(self, *tokens):
        for t in tokens:
            if t is None:
                continue
            if isinstance(t, list):
                self.wait(*t)
                continue
            sem, value = t
            if self.seen.get(sem.name, 0) < value:
                self.seen[sem.name] = value
                self.engine.wait_ge(sem, value)

    def quiet(self, fn, *tokens):
        self.wait(*tokens)
        fn(self.engine)

    def do(self, fn, *tokens):
        self.wait(*tokens)
        self.n += 1
        fn(self.engine).then_inc(self.sem, 1)
        return (self.sem, self.n)

    def last(self):
        return (self.sem, self.n) if self.n else None

    def dma(self, fn, token, *tokens):
        self.wait(*tokens)
        fn(self.engine).then_inc(token[0], 16)
        return token


class Buffers:

    def __init__(self, views):
        self.free = deque((v, None) for v in views)

    def get(self):
        return self.free.popleft()

    def put(self, view, *tokens):
        self.free.append((view, list(tokens)))


def build_program(nc, dram, out):
    fp32, f32r, u8, i32 = mybir.dt.float32, mybir.dt.float32r, mybir.dt.uint8, mybir.dt.int32
    ALU, ACT, AX = mybir.AluOpType, mybir.ActivationFunctionType, mybir.AxisListType
    offs, NP = param_offsets()
    ctx = ExitStack()
    with ctx:
        def sb(name, shape, dt=fp32, stack=ctx):
            return stack.enter_context(nc.sbuf_tensor(name, shape, dt))

        def sem(name):
            return ctx.enter_context(nc.semaphore(name))

        h_sb = sb("h_sb", [128, NT, S])
        yhi = sb("yhi", [128, NT, S], f32r)
        ylo = sb("ylo", [128, NT, S], f32r)
        raw = sb("raw", [128, NRAW, 1024])
        whi = sb("whi", [128, NW, 1024], f32r)
        wlo = sb("wlo", [128, NW, 1024], f32r)
        cst = sb("cst", [128, NCONST])
        msk = sb("msk", [128, 7, 128], u8)
        par = sb("par", [128, NP])
        mod = sb("mod", [128, 168])
        acc = sb("acc", [128, 1024])
        sil = sb("sil", [128, 16])
        coef = sb("coef", [128, 32])
        stat = sb("stat", [128, 4, 32])
        lbc = sb("lbc", [128, 8, 4])
        lamb = sb("lamb", [128, 8])
        tmps = sb("tmps", [128, NTMP, 516])
        banks = [ctx.enter_context(nc.psum_tensor(f"bank{i}", [128, S], fp32)) for i in range(8)]

        T, A, V, G, Y = (Queue(e, sem(f"s_{n}")) for e, n in (
            (nc.tensor, "pe"), (nc.scalar, "act"), (nc.vector, "dve"), (nc.gpsimd, "pool"), (nc.sync, "sp")))
        s_raw = [sem(f"s_raw{i}") for i in range(NRAW)]
        s_par, s_cst, s_x, s_msk = sem("s_par"), sem("s_cst"), sem("s_x"), sem("s_msk")
        s_out = [sem(f"s_out{n}") for n in range(NT)]
        PS = Buffers([b[:, :] for b in banks])
        TM = Buffers([tmps[:, i, :] for i in range(NTMP)])

        ident = cst[:, IDENT:IDENT + 128]
        ones = cst[:, ONES:ONES + 128]
        one = cst[:, ONES:ONES + 1]
        eps = cst[:, EPS_C:EPS_C + 1]

        def pc(name, i=0, n=1, p=128):
            return par[0:p, offs[name] + i:offs[name] + i + n]

        def f(ap):
            return ap.bitcast(fp32)

        def bc(ap, n, axis):
            v = ap.unsqueeze(axis)
            shape = list(v.shape)
            shape[axis] = n
            return v.to_broadcast(shape)

        t_par = Y.dma(lambda e: e.dma_start(par[:, :], dram["par"]), (s_par, 16))
        t_cst = Y.dma(lambda e: e.dma_start(cst[:, :], dram["cst"]), (s_cst, 16))
        t_msk = Y.dma(lambda e: e.dma_start(acc[:, 0:896], dram["msk"]), (s_msk, 16))
        t_msk = V.do(lambda e: e.tensor_copy(msk[:, :, :].rearrange("p n t -> p (n t)"), acc[:, 0:896]), t_msk)
        t_x = A.dma(lambda e: e.dma_start(h_sb[:, :, :], dram["x"]), (s_x, 16))

        lin, ada = [], []

        def add(name, tag, width=1024):
            for i in range(dram[name].shape[0]):
                lin.append((name, i, tag, width))

        for b, n in (("ffn1", 3), ("mix", 0), ("ffn2", 3)):
            if b == "mix":
                for part in ("mqk", "mif", "mv", "hq", "hf", "hi", "mo", "hg", "wout"):
                    add("w_" + part, part)
                continue
            ups = [min(8, F1 // 128 - 8 * g) for g in range(n)]
            for g in range(n):
                add(f"{b}_up{g}", f"{b}_up{g}")
                if g:
                    add(f"{b}_dn{g - 1}", f"{b}_dn{g - 1}", 128 * ups[g - 1])
            add(f"{b}_dn{n - 1}", f"{b}_dn{n - 1}", 128 * ups[n - 1])
        for layer in range(2):
            if layer == 0:
                for part in ("gv", "ga", "gq", "gk", "gr", "go"):
                    add("w_" + part, part)
            else:
                for part in ("dv", "dqk", "do"):
                    add("w_" + part, part)
            b = f"mlp{layer}"
            for g in range(4):
                add(f"{b}_up{g}", f"{b}_up{g}")
                if g:
                    add(f"{b}_dn{g - 1}", f"{b}_dn{g - 1}")
            add(f"{b}_dn3", f"{b}_dn3")
        for v in range(21):
            for kt in range(8):
                ada.append((v, kt))
        stream = [("ada", x) for x in ada[:16]]
        rest = ada[16:]
        for n, u in enumerate(lin):
            stream.append(("lin", u))
            if rest:
                stream.append(("ada", rest.pop(0)))
        state = {"at": 0, "lin": 0, "prepped": deque(), "acc": None, "acc_read": t_msk}
        raw_free = [None] * NRAW
        w_free = [None] * NW
        mod_tok = [None] * 21

        def pump_one():
            n = state["at"]
            state["at"] += 1
            kind, u = stream[n]
            slot = n % NRAW
            token = (s_raw[slot], 16 * (n // NRAW + 1))
            if kind == "ada":
                v, kt = u
                src = dram["ada"][v, kt] if v < 9 else dram["ada_2"][v - 9, kt]
                Y.dma(lambda e: e.dma_start(raw[:, slot, :], src), token, raw_free[slot])
                col = sil[:, kt:kt + 1] if v < 9 else sil[:, 8 + kt:9 + kt]
                if kt == 0:
                    t = V.do(lambda e: e.tensor_scalar(acc[:, :], raw[:, slot, :], col, None, ALU.mult),
                             token, state["sil"], state["acc_read"])
                else:
                    t = V.do(lambda e: e.scalar_tensor_tensor(acc[:, :], raw[:, slot, :], col, acc[:, :],
                                                              ALU.mult, ALU.add), token, state["acc"])
                state["acc"] = raw_free[slot] = t
                if kt == 7:
                    bank, free = PS.get()
                    for j in range(8):
                        mm = (T.do if j == 7 else T.quiet)(
                            lambda e, j=j: e.matmul(bank[:, j:j + 1], acc[:, 128 * j:128 * j + 128], one,
                                                    start=True, stop=True), t, free, t_cst)
                    state["acc_read"] = mm
                    bias = pc("ada_b", 8 * v, 8) if v < 9 else pc("ada_b_2", 8 * (v - 9), 8)
                    mod_tok[v] = V.do(lambda e: e.tensor_tensor(mod[:, 8 * v:8 * v + 8], bank[:, 0:8], bias,
                                                                ALU.add), mm, t_par)
                    PS.put(bank, mod_tok[v])
                return
            name, i, tag, width = u
            src = dram[name][i]
            Y.dma(lambda e: e.dma_start(raw[:, slot, 0:width], src), token, raw_free[slot])
            w = state["lin"] % NW
            state["lin"] += 1
            hi = A.do(lambda e: e.activation(whi[:, w, 0:width], raw[:, slot, 0:width], ACT.Copy),
                      token, w_free[w])
            lo = V.do(lambda e: e.tensor_tensor(wlo[:, w, 0:width], raw[:, slot, 0:width],
                                                f(whi[:, w, 0:width]), ALU.subtract), hi, w_free[w])
            raw_free[slot] = lo
            state["prepped"].append((tag, w, [hi, lo]))

        def pump(ahead):
            while len(state["prepped"]) < ahead and state["at"] < len(stream):
                pump_one()

        def need_mod(v):
            while mod_tok[v] is None:
                pump_one()
            return mod_tok[v]

        def unit(tag):
            pump(NW - 1)
            got, w, toks = state["prepped"].popleft()
            assert got == tag, (got, tag)
            return w, toks

        def used(w, tok):
            w_free[w] = tok
            pump(NW - 1)

        def linear(tag, xh, xl, xtoks):
            w, toks = unit(tag)
            bank, free = PS.get()
            kts = len(xtoks)
            T.wait(free, toks)
            for kt in range(kts):
                wh, wl = whi[:, w, 128 * kt:128 * kt + 128], wlo[:, w, 128 * kt:128 * kt + 128]
                a, b = xh[:, kt, :], xl[:, kt, :]
                first, last = kt == 0, kt == kts - 1
                T.quiet(lambda e, wh=wh, a=a, first=first: e.matmul(bank, wh, a, start=first, stop=False), xtoks[kt])
                T.quiet(lambda e, wh=wh, b=b: e.matmul(bank, wh, b, start=False, stop=False))
                mm = (T.do if last else T.quiet)(
                    lambda e, wl=wl, a=a, last=last: e.matmul(bank, wl, a, start=False, stop=last))
            used(w, mm)
            return bank, mm

        def linear_tokens(tag, xh, xl, xtoks, evac):
            got = [PS.get() for _ in range(4)]
            for kp in range(4):
                w, toks = unit(tag)
                for j in range(4):
                    bank, free = got[j]
                    T.wait(free, toks)
                    for k2 in range(2):
                        kt = 2 * kp + k2
                        wh, wl = whi[:, w, 512 * k2:512 * k2 + 512], wlo[:, w, 512 * k2:512 * k2 + 512]
                        a, b = xh[:, kt, 128 * j:128 * j + 128], xl[:, kt, 128 * j:128 * j + 128]
                        first, last = kt == 0, kt == 7
                        T.quiet(lambda e, bank=bank, wh=wh, a=a, first=first:
                                e.matmul(bank, a, wh, start=first, stop=False), xtoks[kt])
                        T.quiet(lambda e, bank=bank, wh=wh, b=b: e.matmul(bank, b, wh, start=False, stop=False))
                        mm = (T.do if k2 == 1 else T.quiet)(
                            lambda e, bank=bank, wl=wl, a=a, last=last: e.matmul(bank, a, wl, start=False, stop=last))
                    if kp == 3:
                        evac(j, bank, mm)
                used(w, mm)

        def square(src, tok):
            buf, free = TM.get()
            t = A.do(lambda e: e.activation(buf[:, 0:S], src, ACT.Square), tok, free)
            return buf, t

        def add_columns(bank, col, buf, first, last, *toks):
            for j in range(4):
                mm = (T.do if j == 3 else T.quiet)(
                    lambda e, j=j: e.matmul(bank[:, col + j:col + j + 1], buf[:, 128 * j:128 * j + 128], one,
                                            start=first and j == 0, stop=last and j == 3), *toks)
            return mm

        def root(bank, n, tok, scale):
            t = A.do(lambda e: e.activation(stat[:, 0, 0:n], bank[:, 0:n], ACT.Sqrt, bias=eps, scale=scale),
                     tok, state.get("stat_read"))
            PS.put(bank, t)
            return V.do(lambda e: e.reciprocal(stat[:, 1, 0:n], stat[:, 0, 0:n]), t, state.get("stat_read"))

        def spread(col, tok):
            buf, free = TM.get()
            t = V.do(lambda e: e.tensor_tensor(
                buf[:, 0:S].rearrange("p (j t) -> p j t", j=4), bc(ident, 4, 1),
                bc(stat[:, 1, col:col + 4], 128, 2), ALU.mult), tok, free)
            state["stat_read"] = t
            bank, free = PS.get()
            mm = T.do(lambda e: e.matmul(bank, ones, buf[:, 0:S], start=True, stop=True), t, free)
            TM.put(buf, mm)
            return bank, mm

        def rms(tiles, toks):
            bank, free = PS.get()
            n = len(tiles)
            for i in range(n):
                buf, t = square(tiles[i], toks[i])
                mm = add_columns(bank, 0, buf, i == 0, i == n - 1, t, free, t_cst)
                TM.put(buf, mm)
            return spread(0, root(bank, 4, mm, 1.0 / D))

        htok = [t_x] * NT
        h_read = [None] * NT
        y_free = [None]

        def split(dst_hi, dst_lo, src, tok, *free):
            hi = A.do(lambda e: e.activation(dst_hi, src, ACT.Copy), tok, *free)
            lo = V.do(lambda e: e.tensor_tensor(dst_lo, src, f(dst_hi), ALU.subtract), hi, *free)
            return [hi, lo]

        def prenorm(g, v_shift, v_scale):
            R, r_tok = rms([h_sb[:, n, :] for n in range(NT)], htok)
            need_mod(v_shift)
            m = need_mod(v_scale)
            A_c = coef[:, 0:8]
            c_tok = V.do(lambda e: e.scalar_tensor_tensor(A_c, mod[:, 8 * v_scale:8 * v_scale + 8], 1.0, g,
                                                          ALU.add, ALU.mult), m, t_par, state.get("coef_read"))
            ytok = []
            pend = []

            def low(n, buf, hi):
                sh = mod[:, 8 * v_shift + n:8 * v_shift + n + 1]
                lo = V.do(lambda e: e.scalar_tensor_tensor(ylo[:, n, :], buf[:, 0:S], sh, f(yhi[:, n, :]),
                                                           ALU.add, ALU.subtract), hi)
                TM.put(buf, lo)
                ytok.append([hi, lo])

            for n in range(NT):
                buf, free = TM.get()
                t = V.do(lambda e, n=n, buf=buf: e.scalar_tensor_tensor(
                    buf[:, 0:S], h_sb[:, n, :], A_c[:, n:n + 1], R, ALU.mult, ALU.mult),
                    c_tok, r_tok, free, htok[n], y_free[0])
                sh = mod[:, 8 * v_shift + n:8 * v_shift + n + 1]
                hi = A.do(lambda e, n=n, buf=buf, sh=sh: e.activation(yhi[:, n, :], buf[:, 0:S], ACT.Identity,
                                                                     bias=sh), t, y_free[0], mod_tok[v_shift])
                h_read[n] = t
                pend.append((n, buf, hi))
                if len(pend) > 1:
                    low(*pend.pop(0))
            low(*pend.pop(0))
            state["coef_read"] = t
            PS.put(R, t)
            return ytok

        def postnorm(tiles, toks, g, v_gate, half):
            R, r_tok = rms(tiles, toks)
            m = need_mod(v_gate)
            C = coef[:, 8:16]
            c_tok = V.do(lambda e: e.scalar_tensor_tensor(C, mod[:, 8 * v_gate:8 * v_gate + 8], half, g,
                                                          ALU.mult, ALU.mult), m, t_par, state.get("coef_read"))
            for n in range(NT):
                buf, free = TM.get()
                t = V.do(lambda e, n=n, buf=buf: e.scalar_tensor_tensor(
                    buf[:, 0:S], tiles[n], C[:, n:n + 1], R, ALU.mult, ALU.mult), c_tok, r_tok, free, toks[n])
                htok[n] = G.do(lambda e, n=n, buf=buf: e.tensor_tensor(h_sb[:, n, :], h_sb[:, n, :], buf[:, 0:S],
                                                                      ALU.add), t, htok[n], h_read[n])
                TM.put(buf, htok[n])
            state["coef_read"] = t
            PS.put(R, t)

        def ffn(name, ytok, counts, gated, result):
            with ExitStack() as st:
                ahi = [sb(f"{name}_ahi{i}", [128, 8, S], f32r, st) for i in range(2)]
                alo = [sb(f"{name}_alo{i}", [128, 8, S], f32r, st) for i in range(2)]
                a_free = [state.get("phase"), state.get("phase")]
                atok = {}

                def up(g):
                    toks = []
                    for i in range(counts[g]):
                        b1, t1 = linear(f"{name}_up{g}", yhi, ylo, ytok)
                        buf, free = TM.get()
                        if gated:
                            t = A.do(lambda e: e.activation(buf[:, 0:S], b1, ACT.Silu), t1, free)
                            PS.put(b1, t)
                            b2, t2 = linear(f"{name}_up{g}", yhi, ylo, ytok)
                            p = V.do(lambda e: e.tensor_tensor(buf[:, 0:S], buf[:, 0:S], b2, ALU.mult), t, t2)
                            PS.put(b2, p)
                        else:
                            t = A.do(lambda e: e.activation(buf[:, 0:S], b1, ACT.Relu), t1, free)
                            PS.put(b1, t)
                            p = V.do(lambda e: e.tensor_tensor(buf[:, 0:S], buf[:, 0:S], buf[:, 0:S], ALU.mult), t)
                        toks.append(split(ahi[g % 2][:, i, :], alo[g % 2][:, i, :], buf[:, 0:S], p, a_free[g % 2]))
                        TM.put(buf, toks[-1])
                    atok[g] = toks
                    y_free[0] = T.last()

                def down(g):
                    for n in range(NT):
                        bank, t = linear(f"{name}_dn{g}", ahi[g % 2], alo[g % 2], atok[g])
                        PS.put(bank, result(g, n, bank, t))
                    a_free[g % 2] = T.last()

                up(0)
                for g in range(1, len(counts)):
                    up(g)
                    down(g - 1)
                down(len(counts) - 1)

        def phase_end():
            state["phase"] = [t for t in (T.last(), A.last(), V.last(), G.last()) if t]

        def gated_ffn(name, ytok, g_post, v_gate):
            with ExitStack() as st:
                yac = sb(f"{name}_y", [128, NT, S], fp32, st)
                toks = [state.get("phase")] * NT

                def result(g, n, bank, t):
                    if g == 0:
                        toks[n] = A.do(lambda e: e.activation(yac[:, n, :], bank, ACT.Copy), t, toks[n])
                    else:
                        toks[n] = V.do(lambda e: e.tensor_tensor(yac[:, n, :], yac[:, n, :], bank, ALU.add),
                                       t, toks[n])
                    return toks[n]

                ffn(name, ytok, [8, 8, 6], True, result)
                postnorm([yac[:, n, :] for n in range(NT)], toks, g_post, v_gate, 0.5)
            phase_end()

        def add_gated(v_gate):
            m = need_mod(v_gate)

            def result(g, n, bank, t):
                htok[n] = V.do(lambda e: e.scalar_tensor_tensor(
                    h_sb[:, n, :], bank, mod[:, 8 * v_gate + n:8 * v_gate + n + 1], h_sb[:, n, :],
                    ALU.mult, ALU.add), t, m, htok[n], h_read[n])
                return htok[n]
            return result

        def decay_attention(q, k, fd, tb, attd, atto, qt, kt_, ft, masked, bg):
            cur, nxt = fd, tb
            tt = list(ft)
            ad = [None] * 4
            ao = [[] for _ in range(4)]

            def scores(h):
                bank, free = PS.get()
                for j in range(4):
                    c = slice(128 * j, 128 * j + 128)
                    mm = (T.do if j == 3 else T.quiet)(
                        lambda e, c=c: e.matmul(bank[:, c], k[:, h, c], q[:, h, c], start=True, stop=True),
                        qt[h], kt_[h], free)
                return bank, mm

            def d4(ap):
                return ap.rearrange("p (j t) -> p j t", j=4)

            for h in range(4):
                bank, mm = scores(h)
                ad[h] = V.do(lambda e: e.tensor_tensor(attd[:, h, :, :], d4(bank), bc(ident, 4, 1), ALU.mult),
                             mm, masked)
                PS.put(bank, ad[h])
                qt[h] = V.do(lambda e: e.tensor_tensor(q[:, h, :], q[:, h, :], fd[:, h, 0:S], ALU.mult),
                             mm, qt[h], ft[h])
            bg()
            for n, hh in enumerate(LEVELS + [128, 256]):
                nb = S // (2 * hh)
                for h in range(4):
                    if hh <= 64:
                        bank, mm = scores(h)
                        ad[h] = V.do(lambda e: e.copy_predicated(attd[:, h, :, :], bc(msk[:, n, :], 4, 1),
                                                                 d4(bank)), mm, ad[h], t_msk)
                        PS.put(bank, ad[h])
                    elif hh == 128:
                        bank, free = PS.get()
                        T.quiet(lambda e: e.matmul(bank[:, 0:128], k[:, h, 0:128], q[:, h, 128:256],
                                                   start=True, stop=True), qt[h], kt_[h], free)
                        mm = T.do(lambda e: e.matmul(bank[:, 128:256], k[:, h, 256:384], q[:, h, 384:512],
                                                     start=True, stop=True))
                        ao[h] += [A.do(lambda e: e.activation(atto[:, h, 0:128], bank[:, 0:128], ACT.Copy),
                                       mm, masked),
                                  A.do(lambda e: e.activation(atto[:, h, 640:768], bank[:, 128:256], ACT.Copy),
                                       mm, masked)]
                        PS.put(bank, ao[h][-1])
                    else:
                        bank, free = PS.get()
                        T.quiet(lambda e: e.matmul(bank[:, 0:256], k[:, h, 0:128], q[:, h, 256:512],
                                                   start=True, stop=True), qt[h], kt_[h], free)
                        mm = T.do(lambda e: e.matmul(bank[:, 256:512], k[:, h, 128:256], q[:, h, 256:512],
                                                     start=True, stop=True))
                        ao[h] += [A.do(lambda e: e.activation(atto[:, h, 128:640], bank, ACT.Copy), mm, masked)]
                        PS.put(bank, ao[h][-1])
                    if hh == 256:
                        continue
                    qv = q[:, h, :].rearrange("p (b x i) -> p b x i", x=2, i=hh)[:, :, 1, :]
                    kv = k[:, h, :].rearrange("p (b x i) -> p b x i", x=2, i=hh)[:, :, 0, :]
                    tv = cur[:, h, 0:2 * nb].rearrange("p (b x) -> p b x", x=2)
                    t1 = V.do(lambda e: e.tensor_tensor(qv, qv, bc(tv[:, :, 0], hh, 2), ALU.mult),
                              mm, qt[h], tt[h])
                    kt_[h] = G.do(lambda e: e.tensor_tensor(kv, kv, bc(tv[:, :, 1], hh, 2), ALU.mult),
                                  mm, kt_[h], tt[h])
                    qt[h] = t1
                    w = [kt_prev for kt_prev in (state["kread"].get(h),) if kt_prev]
                    tt[h] = V.do(lambda e: e.tensor_tensor(nxt[:, h, 0:nb], tv[:, :, 0], tv[:, :, 1], ALU.mult),
                                 tt[h], t1, *w)
                    state["kread"][h] = kt_[h]
                cur, nxt = nxt, cur
                bg()
            return ad, ao

        def mix_values(h, vals, col, attd, atto, toks):
            bank, free = PS.get()
            at = 0
            T.wait(free, toks)
            for j in range(4):
                v = vals[:, j, col:col + 128]
                last = j == 3
                mm = (T.do if last else T.quiet)(
                    lambda e, j=j, v=v, last=last: e.matmul(bank[:, 128 * j:128 * j + 128], v, attd[:, h, j, :],
                                                            start=j == 0, stop=last))
                if not last:
                    w = 384 - 128 * j
                    T.quiet(lambda e, j=j, v=v, at=at, w=w: e.matmul(
                        bank[:, 128 * (j + 1):512], v, atto[:, h, at:at + w], start=False, stop=False))
                    at += w
            return bank, mm

        t = A.do(lambda e: e.activation(sil[:, 0:16], pc("c", 0, 16), ACT.Silu), t_par)
        state["sil"] = t

        ytok = prenorm(pc("ffn1_pre_g", 0, 8), 0, 1)
        gated_ffn("ffn1", ytok, pc("ffn1_post_g", 0, 8), 2)

        ytok = prenorm(pc("mix_pre_g", 0, 8), 3, 4)
        with ExitStack() as st:
            ph = state["phase"]
            mqk = sb("mqk", [128, 8, S], fp32, st)
            vals = sb("vals", [128, 4, S], fp32, st)
            hq = sb("hq", [128, 4, S], fp32, st)
            hf = sb("hf", [128, 4, S], fp32, st)
            hk = sb("hk", [128, 4, S], fp32, st)
            hg = sb("hg", [128, 4, S], fp32, st)
            attd = sb("attd", [128, 4, 4, 128], fp32, st)
            atto = sb("atto", [128, 4, 768], fp32, st)
            tb = sb("tb", [128, 4, 256], fp32, st)
            mo = mqk[:, 4:8, :]

            l0, l1 = pc("hgrn_lb_logits", 0, 4), pc("hgrn_lb_logits", 4, 4)
            t = V.do(lambda e: e.tensor_tensor(lbc[:, 0, :], l0, l1, ALU.max), t_par)
            t1 = V.do(lambda e: e.tensor_tensor(lbc[:, 1, :], l0, lbc[:, 0, :], ALU.subtract), t)
            t2 = V.do(lambda e: e.tensor_tensor(lbc[:, 2, :], l1, lbc[:, 0, :], ALU.subtract), t)
            t = A.do(lambda e: e.activation(lbc[:, 3:5, :], lbc[:, 1:3, :], ACT.Exp), t1, t2)
            t = V.do(lambda e: e.tensor_tensor(lbc[:, 5, :], lbc[:, 3, :], lbc[:, 4, :], ALU.add), t)
            t = V.do(lambda e: e.reciprocal(lbc[:, 6, :], lbc[:, 5, :]), t)
            t = V.do(lambda e: e.tensor_tensor(lbc[:, 7, :], lbc[:, 3, :], lbc[:, 6, :], ALU.mult), t)
            lb_tok = V.do(lambda e: e.tensor_scalar(lbc[:, 0, :], lbc[:, 7, :], -1.0, 1.0, ALU.mult, ALU.add), t)

            qk_tok = []
            for i in range(8):
                bank, t = linear("mqk", yhi, ylo, ytok)
                cb, free = TM.get()
                z = V.do(lambda e: e.memset(cb[:, 0:3], 0.0), free)
                t = A.do(lambda e: e.activation(cb[:, 3:3 + S], bank, ACT.Copy), t, free)
                PS.put(bank, t)
                w = [pc("mlstm_conv_w", 8 * j + i) for j in range(4)]
                a = mqk[:, i, :]
                t = V.do(lambda e: e.tensor_scalar(a, cb[:, 0:S], w[0], None, ALU.mult), t, z, ph, t_par)
                for j in range(1, 4):
                    t = V.do(lambda e, j=j: e.scalar_tensor_tensor(a, cb[:, j:j + S], w[j], a, ALU.mult, ALU.add), t)
                TM.put(cb, t)
                qk_tok.append(A.do(lambda e: e.activation(a, a, ACT.Silu, bias=pc("mlstm_conv_b", i)), t))
            bank, t = linear("mif", yhi, ylo, ytok)
            gts, gfree = TM.get()
            g_tok = A.do(lambda e: e.activation(gts[0:8, 0:S], bank[0:8, :], ACT.Identity,
                                                bias=pc("mlstm_gate_b", 0, 1, 8)), t, gfree, t_par)
            PS.put(bank, g_tok)
            v_tok = [None] * 4

            def keep_v(j, bank, t):
                v_tok[j] = A.do(lambda e: e.activation(vals[:, j, :], bank, ACT.Copy), t, ph)
                PS.put(bank, v_tok[j])

            linear_tokens("mv", yhi, ylo, ytok, keep_v)

            bank, free = PS.get()
            mm = T.do(lambda e: e.matmul(bank[0:4, :], cst[0:8, SEL_C:SEL_C + 4], gts[0:8, 0:S],
                                         start=True, stop=True), g_tok, free, t_cst)
            lf, lfree = TM.get()
            w1, w1free = TM.get()
            t = A.do(lambda e: e.activation(w1[0:4, 0:S], bank[0:4, :], ACT.Abs), mm, w1free)
            t = A.do(lambda e: e.activation(w1[0:4, 0:S], w1[0:4, 0:S], ACT.Exp, scale=-1.0), t)
            t = A.do(lambda e: e.activation(w1[0:4, 0:S], w1[0:4, 0:S], ACT.Ln, bias=1.0), t)
            t = V.do(lambda e: e.scalar_tensor_tensor(lf[0:4, 0:S], bank[0:4, :], 0.0, w1[0:4, 0:S],
                                                      ALU.min, ALU.subtract), t, lfree)
            PS.put(bank, t)
            z = V.do(lambda e: e.memset(w1[0:4, 0:S], 1.0), t)
            bsum, bfree = TM.get()
            t = V.do(lambda e: e.tensor_tensor_scan(bsum[0:4, 0:S], w1[0:4, 0:S], lf[0:4, 0:S], 0.0,
                                                    ALU.mult, ALU.add), t, z, bfree)
            u_tok = V.do(lambda e: e.tensor_tensor(gts[0:4, 0:S], gts[0:4, 0:S], bsum[0:4, 0:S], ALU.subtract), t, mm)
            m_tok = V.do(lambda e: e.tensor_tensor_scan(lf[0:4, 0:S], w1[0:4, 0:S], gts[0:4, 0:S], -BIG,
                                                        ALU.mult, ALU.max), u_tok)
            mt_tok = V.do(lambda e: e.tensor_tensor(bsum[0:4, 0:S], bsum[0:4, 0:S], lf[0:4, 0:S], ALU.add), m_tok)
            TM.put(w1, m_tok)
            bank, free = PS.get()
            T.wait(u_tok, mt_tok, free)
            for j in range(4):
                T.quiet(lambda e, j=j: e.matmul(bank[:, 4 * j:4 * j + 4], gts[0:4, 128 * j:128 * j + 128],
                                                cst[0:4, IDENT:IDENT + 4], start=True, stop=True))
                mm = T.do(lambda e, j=j: e.matmul(bank[:, 16 + 4 * j:20 + 4 * j], bsum[0:4, 128 * j:128 * j + 128],
                                                  cst[0:4, IDENT:IDENT + 4], start=True, stop=True))
            uc = stat[:, 2, 0:16]
            em = stat[:, 2, 16:32]
            uc_tok = V.do(lambda e: e.tensor_copy(uc, bank[:, 0:16]), mm)
            em_tok = A.do(lambda e: e.activation(em, bank[:, 16:32], ACT.Exp, scale=-1.0), mm, uc_tok)
            PS.put(bank, uc_tok, em_tok)
            TM.put(gts, mm)
            TM.put(bsum, mm)

            attd2 = attd[:, :, :, :].rearrange("p h j t -> p (h j t)")
            atto2 = atto[:, :, :].rearrange("p h t -> p (h t)")
            hg2 = hg[:, :, :].rearrange("p h t -> p (h t)")
            starts = [0, 512, 896, 1152]
            q_toks = [None] * 4
            fg_tok = [None] * 4
            fk_tok = [None] * 4

            def unit_hq(i):
                bank, t = linear("hq", yhi, ylo, ytok)
                q_toks[i] = A.do(lambda e: e.activation(hq[:, i, :], bank, ACT.Silu), t, ph)
                PS.put(bank, q_toks[i])

            def unit_hf(i):
                bank, t = linear("hf", yhi, ylo, ytok)
                t = A.do(lambda e: e.activation(hf[:, i, :], bank, ACT.Sigmoid), t, ph)
                PS.put(bank, t)
                fg_tok[i] = V.do(lambda e: e.tensor_scalar(hf[:, i, :], hf[:, i, :], lbc[:, 0, i:i + 1],
                                                           lbc[:, 7, i:i + 1], ALU.mult, ALU.add), t, lb_tok)
                fk_tok[i] = V.do(lambda e: e.tensor_scalar(hk[:, i, :], hf[:, i, :], -1.0, 1.0, ALU.mult, ALU.add),
                                 fg_tok[i], ph)

            todo = deque([lambda i=i: unit_hq(i) for i in range(4)] + [lambda i=i: unit_hf(i) for i in range(4)])
            den, dfree = PS.get()
            T.wait(dfree)
            w_read, x_read = [None, None], [None, None]
            n_tok = []
            sq_scale = 128.0 ** -0.5
            for h in range(4):
                W = attd2[:, 0:1280] if h % 2 == 0 else atto2[:, 1280:2560]
                X = atto2[:, 0:1280] if h % 2 == 0 else hg2[:, 0:1280]
                bank, free = PS.get()
                mm = T.do(lambda e: e.matmul(bank, cst[0:4, IDENT + h:IDENT + h + 1].to_broadcast([4, 128]),
                                             lf[0:4, 0:S], start=True, stop=True), m_tok, free)
                dm, dmfree = TM.get()
                t = V.do(lambda e: e.tensor_tensor(dm[:, 0:S].rearrange("p (j t) -> p j t", j=4),
                                                   bank.rearrange("p (j t) -> p j t", j=4),
                                                   bc(cst[:, CAUS:CAUS + 128], 4, 1), ALU.add), mm, dmfree)
                wt = []
                for j in range(4):
                    a, bias = starts[j], uc[:, 4 * j + h:4 * j + h + 1]
                    Wj = W[:, a:a + 512 - 128 * j]
                    wt.append(A.do(lambda e, j=j, Wj=Wj, bias=bias: e.activation(
                        Wj[:, 0:128], dm[:, 128 * j:128 * j + 128], ACT.Exp, bias=bias, scale=-1.0),
                        t, uc_tok, ph, w_read[h % 2]))
                    if j < 3:
                        wt[-1] = A.do(lambda e, j=j, Wj=Wj, bias=bias: e.activation(
                            Wj[:, 128:512 - 128 * j], bank[:, 128 * j + 128:512], ACT.Exp, bias=bias, scale=-1.0), mm)
                PS.put(bank, t, wt[-1])
                TM.put(dm, wt[-1])
                st_ = []
                for j in range(4):
                    a, wd = starts[j], 512 - 128 * j
                    sbank, free = PS.get()
                    mm = T.do(lambda e, j=j, sbank=sbank, wd=wd: e.matmul(
                        sbank[:, 0:wd], mqk[:, 4 + h, 128 * j:128 * j + 128], mqk[:, h, 128 * j:512],
                        start=True, stop=True), qk_tok[h], qk_tok[4 + h], free)
                    st_.append(V.do(lambda e, a=a, wd=wd, sbank=sbank: e.scalar_tensor_tensor(
                        X[:, a:a + wd], sbank[:, 0:wd], sq_scale, W[:, a:a + wd], ALU.mult, ALU.mult),
                        mm, wt, x_read[h % 2], ph))
                    PS.put(sbank, st_[-1])
                w_read[h % 2] = st_[-1]
                bank, free = PS.get()
                T.wait(free, v_tok, st_)
                for j in range(4):
                    a, wd = starts[j], 512 - 128 * j
                    T.quiet(lambda e, j=j, a=a, wd=wd: e.matmul(
                        bank[:, 128 * j:512], vals[:, j, 128 * h:128 * h + 128], X[:, a:a + wd],
                        start=j == 0, stop=j == 3))
                for j in range(4):
                    for i in range(j, 4):
                        a = starts[j] + 128 * (i - j)
                        mm = (T.do if (i, j) == (3, 3) else T.quiet)(
                            lambda e, i=i, j=j, a=a: e.matmul(
                                den[:, 4 * h + i:4 * h + i + 1], X[:, a:a + 128], one,
                                start=(h, i, j) == (0, 0, 0), stop=(h, i, j) == (3, 3, 3)))
                x_read[h % 2] = mm
                n_tok.append(A.do(lambda e: e.activation(mqk[:, h, :], bank, ACT.Copy), mm))
                PS.put(bank, n_tok[-1])
                for _ in range(2):
                    todo.popleft()()
            TM.put(lf, T.last())
            mls_end = [w_read[1], x_read[1]]
            t = A.do(lambda e: e.activation(stat[:, 3, 0:16], den[:, 0:16], ACT.Abs), mm)
            PS.put(den, t)
            emv = em.rearrange("p (j h) -> p h j", j=4)
            dv = stat[:, 3, 0:16].rearrange("p (h j) -> p h j", h=4)
            t = V.do(lambda e: e.tensor_tensor(dv, dv, emv, ALU.max), t, em_tok)
            t = V.do(lambda e: e.tensor_scalar(stat[:, 3, 0:16], stat[:, 3, 0:16], 1e18, None, ALU.min), t)
            d2_tok = V.do(lambda e: e.scalar_tensor_tensor(stat[:, 3, 0:16], stat[:, 3, 0:16], EPS,
                                                           stat[:, 3, 0:16], ALU.mult, ALU.mult), t)

            hv_tok = [None] * 4

            def keep_hv(j, bank, t):
                hv_tok[j] = A.do(lambda e: e.activation(vals[:, j, :], bank, ACT.Copy), t, mls_end)
                PS.put(bank, hv_tok[j])

            linear_tokens("hi", yhi, ylo, ytok, keep_hv)
            mo_tok, hg_tok = [None] * 4, [None] * 4

            def unit_mo(i):
                bank, t = linear("mo", yhi, ylo, ytok)
                mo_tok[i] = A.do(lambda e: e.activation(mo[:, i, :], bank, ACT.Sigmoid), t, mls_end)
                PS.put(bank, mo_tok[i])

            def unit_hg(i):
                bank, t = linear("hg", yhi, ylo, ytok)
                hg_tok[i] = A.do(lambda e: e.activation(hg[:, i, :], bank, ACT.Silu), t, mls_end)
                PS.put(bank, hg_tok[i])

            todo = deque([lambda i=i: unit_mo(i) for i in range(4)] + [lambda i=i: unit_hg(i) for i in range(4)])

            def bg():
                if todo:
                    todo.popleft()()

            state["kread"] = {}
            ad, ao = decay_attention(hq, hk, hf, tb, attd, atto, q_toks, fk_tok, fg_tok, mls_end, bg)
            while todo:
                bg()
            y_read = T.last()
            o_tok = []
            for h in range(4):
                bank, t = mix_values(h, vals, 128 * h, attd, atto, [hv_tok, ad[h], ao[h]])
                o_tok.append(A.do(lambda e: e.activation(hq[:, h, :], bank, ACT.Copy), t))
                PS.put(bank, o_tok[-1])

            bank, free = PS.get()
            num = [mqk[:, h, :] for h in range(4)] + [hq[:, h, :] for h in range(4)]
            num_tok = n_tok + o_tok
            gate = [mo[:, h, :] for h in range(4)] + [hg[:, h, :] for h in range(4)]
            gate_tok = mo_tok + hg_tok
            for h in range(8):
                buf, t = square(num[h], num_tok[h])
                mm = add_columns(bank, 4 * h, buf, h == 0, h == 7, t, free)
                TM.put(buf, mm)
            ta = V.do(lambda e: e.scalar_tensor_tensor(stat[:, 0, 0:16], bank[:, 0:16], 1 / 128, stat[:, 3, 0:16],
                                                       ALU.mult, ALU.add), mm, d2_tok, state.get("stat_read"))
            tb_ = V.do(lambda e: e.tensor_scalar(stat[:, 0, 16:32], bank[:, 16:32], 1 / 128, EPS, ALU.mult, ALU.add), mm)
            PS.put(bank, tb_)
            t = A.do(lambda e: e.activation(stat[:, 0, 0:32], stat[:, 0, 0:32], ACT.Sqrt), ta, tb_)
            r_tok = V.do(lambda e: e.reciprocal(stat[:, 1, 0:32], stat[:, 0, 0:32]), t)
            x_tok = []
            for h in range(8):
                R, t = spread(4 * h, r_tok)
                g = pc("mlstm_norm_g", h) if h < 4 else pc("hgrn_norm_g", h - 4)
                buf, free = TM.get()
                t = V.do(lambda e: e.scalar_tensor_tensor(buf[:, 0:S], num[h], g, R, ALU.mult, ALU.mult),
                         t, free, num_tok[h])
                PS.put(R, t)
                t = G.do(lambda e: e.tensor_tensor(buf[:, 0:S], buf[:, 0:S], gate[h], ALU.mult), t, gate_tok[h])
                x_tok.append(split(yhi[:, h, :], ylo[:, h, :], buf[:, 0:S], t, y_read))
                TM.put(buf, x_tok[-1])
            tiles, toks = [], []
            for n in range(NT):
                bank, t = linear("wout", yhi, ylo, x_tok)
                dst = attd[:, n, :, :].rearrange("p j t -> p (j t)") if n < 4 else hk[:, n - 4, :]
                t = A.do(lambda e: e.activation(dst, bank, ACT.Copy), t, o_tok)
                PS.put(bank, t)
                tiles.append(dst)
                toks.append(t)
            y_free[0] = T.last()
            postnorm(tiles, toks, pc("mix_post_g", 0, 8), 5, 1.0)
        phase_end()

        ytok = prenorm(pc("ffn2_pre_g", 0, 8), 6, 7)
        gated_ffn("ffn2", ytok, pc("ffn2_post_g", 0, 8), 8)

        ytok = prenorm(pc("norm_g_2", 0, 8), 9, 10)
        with ExitStack() as st:
            ph = state["phase"]
            qk = sb("gqk", [128, 8, S], fp32, st)
            q, k = qk[:, 0:4, :], qk[:, 4:8, :]
            fd = sb("gf", [128, 4, S], fp32, st)
            vals = sb("gvals", [128, 4, D], fp32, st)
            rg = sb("grg", [128, 8, S], fp32, st)
            attd = sb("gattd", [128, 4, 4, 128], fp32, st)
            atto = sb("gatto", [128, 4, 768], fp32, st)
            tb = sb("gtb", [128, 4, 256], fp32, st)
            v_tok = []

            for half in range(2):
                def keep_v(j, bank, t):
                    v_tok.append(A.do(lambda e: e.activation(vals[:, j, 512 * half:512 * half + 512], bank, ACT.Copy),
                                      t, ph))
                    PS.put(bank, v_tok[-1])
                linear_tokens("gv", yhi, ylo, ytok, keep_v)
            bank, t = linear("ga", yhi, ylo, ytok)
            alr, free = TM.get()
            t_a = A.do(lambda e: e.activation(alr[0:16, 0:S], bank[0:16, :], ACT.Copy), t, free)
            PS.put(bank, t_a)
            ga2, free2 = TM.get()
            s_a2 = sem("s_a2")
            t_a2 = Y.dma(lambda e: e.dma_start(ga2[0:16, 0:S], dram["a2"]), (s_a2, 16), free2)
            qt, kt_, ft = [], [], []
            for i in range(4):
                bank, t = linear("gq", yhi, ylo, ytok)
                qt.append(A.do(lambda e: e.activation(q[:, i, :], bank, ACT.Copy, scale=128.0 ** -0.5), t, ph))
                PS.put(bank, qt[-1])
            for i in range(4):
                bank, free = PS.get()
                mm = T.do(lambda e: e.matmul(bank, ga2[0:16, 128 * i:128 * i + 128], alr[0:16, 0:S],
                                             start=True, stop=True), t_a, t_a2, free)
                z, zfree = TM.get()
                l, lfree = TM.get()
                t = A.do(lambda e: e.activation(z[:, 0:S], bank, ACT.Identity, bias=pc("gla_b_a_2", i)), mm, zfree)
                PS.put(bank, t)
                t1 = A.do(lambda e: e.activation(l[:, 0:S], z[:, 0:S], ACT.Abs), t, lfree)
                t1 = A.do(lambda e: e.activation(l[:, 0:S], l[:, 0:S], ACT.Exp, scale=-1.0), t1)
                t1 = A.do(lambda e: e.activation(l[:, 0:S], l[:, 0:S], ACT.Ln, bias=1.0), t1)
                t1 = V.do(lambda e: e.scalar_tensor_tensor(z[:, 0:S], z[:, 0:S], 0.0, l[:, 0:S],
                                                           ALU.min, ALU.subtract), t1)
                ft.append(A.do(lambda e: e.activation(fd[:, i, :], z[:, 0:S], ACT.Exp, scale=1 / 16), t1, ph))
                TM.put(z, ft[-1])
                TM.put(l, t1)
            TM.put(alr, mm)
            TM.put(ga2, mm)
            for i in range(4):
                bank, t = linear("gk", yhi, ylo, ytok)
                kt_.append(A.do(lambda e: e.activation(k[:, i, :], bank, ACT.Copy), t, ph))
                PS.put(bank, kt_[-1])
            r_toks = [None] * 8

            def unit_r(i):
                bank, t = linear("gr", yhi, ylo, ytok)
                r_toks[i] = A.do(lambda e: e.activation(rg[:, i, :], bank, ACT.Silu, bias=pc("gla_b_r_2", i)), t, ph)
                PS.put(bank, r_toks[i])

            todo2 = deque([lambda i=i: unit_r(i) for i in range(8)])

            def bg2():
                if todo2:
                    todo2.popleft()()

            state["kread"] = {}
            ad, ao = decay_attention(q, k, fd, tb, attd, atto, qt, kt_, ft, ph, bg2)
            while todo2:
                bg2()
            y_read = T.last()
            o_tok = []
            for i in range(8):
                bank, t = mix_values(i // 2, vals, 128 * i, attd, atto, [v_tok, ad[i // 2], ao[i // 2]])
                o_tok.append(A.do(lambda e: e.activation(qk[:, i, :], bank, ACT.Copy), t, y_read))
                PS.put(bank, o_tok[-1])
            bank, free = PS.get()
            for i in range(8):
                buf, t = square(qk[:, i, :], o_tok[i])
                for j in range(4):
                    mm = (T.do if j == 3 else T.quiet)(
                        lambda e, i=i, j=j, buf=buf: e.matmul(
                            bank[:, 4 * (i // 2) + j:4 * (i // 2) + j + 1], buf[:, 128 * j:128 * j + 128], one,
                            start=(i, j) == (0, 0), stop=(i, j) == (7, 3)), t, free)
                TM.put(buf, mm)
            r_tok = root(bank, 16, mm, 1.0 / 256)
            x_tok = []
            for h in range(4):
                R, t_r = spread(4 * h, r_tok)
                for e2 in range(2):
                    i = 2 * h + e2
                    buf, free = TM.get()
                    t = V.do(lambda e: e.scalar_tensor_tensor(buf[:, 0:S], qk[:, i, :], pc("gla_norm_g_2", e2), R,
                                                              ALU.mult, ALU.mult), t_r, free, o_tok[i])
                    if e2:
                        PS.put(R, t)
                    t = G.do(lambda e: e.tensor_tensor(buf[:, 0:S], buf[:, 0:S], rg[:, i, :], ALU.mult), t, r_toks[i])
                    x_tok.append(split(yhi[:, i, :], ylo[:, i, :], buf[:, 0:S], t, y_read))
                    TM.put(buf, x_tok[-1])
            result = add_gated(11)
            for n in range(NT):
                bank, t = linear("go", yhi, ylo, x_tok)
                PS.put(bank, result(0, n, bank, t))
            y_free[0] = T.last()
        phase_end()

        ytok = prenorm(pc("norm_g_2", 8, 8), 12, 13)
        ffn("mlp0", ytok, [8] * 4, False, add_gated(14))
        phase_end()

        ytok = prenorm(pc("norm_g_2", 16, 8), 15, 16)
        with ExitStack() as st:
            ph = state["phase"]
            qs = sb("dq", [128, 8, S], fp32, st)
            ks = sb("dk", [128, 8, S], fp32, st)
            vals = sb("dvals", [128, 4, D], fp32, st)
            cosr = sb("cosr", [128, S], fp32, st)
            sinr = sb("sinr", [128, S], fp32, st)
            pp = sb("dp", [128, 2, 2, S], fp32, st)
            aT = sb("daT", [128, 2, S], fp32, st)
            sm = sb("dsm", [128, 2, 8], fp32, st)
            posi = sb("posi", [128, S], i32, st)
            s_pos = sem("s_pos")
            t_pos = Y.dma(lambda e: e.dma_start(posi[:, :], dram["pos"]), (s_pos, 16), ph)

            ang, af = TM.get()
            kf, kff = TM.get()
            t = V.do(lambda e: e.tensor_copy(ang[:, 0:S], posi[:, :]), t_pos, af)
            t = V.do(lambda e: e.tensor_scalar(ang[:, 0:S], ang[:, 0:S], cst[:, INVF_C:INVF_C + 1], None, ALU.mult), t)
            t = V.do(lambda e: e.tensor_scalar(kf[:, 0:S], ang[:, 0:S], 1 / (2 * math.pi), MAGIC, ALU.mult, ALU.add),
                     t, kff)
            t = V.do(lambda e: e.tensor_scalar(kf[:, 0:S], kf[:, 0:S], MAGIC, None, ALU.subtract), t)
            for part in (PI_A, PI_B, PI_C):
                t = V.do(lambda e, part=part: e.scalar_tensor_tensor(ang[:, 0:S], kf[:, 0:S], -part, ang[:, 0:S],
                                                                     ALU.mult, ALU.add), t)
            t = V.do(lambda e: e.tensor_scalar(ang[:, 0:S], ang[:, 0:S], -3.1415925, 3.1415925, ALU.max, ALU.min), t)
            s_tok = A.do(lambda e: e.activation(sinr[:, :], ang[:, 0:S], ACT.Sin), t, ph)
            t = A.do(lambda e: e.activation(kf[:, 0:S], ang[:, 0:S], ACT.Abs), t)
            c_tok = A.do(lambda e: e.activation(cosr[:, :], kf[:, 0:S], ACT.Sin, bias=cst[:, HPI_C:HPI_C + 1],
                                                scale=-1.0), t, ph)
            TM.put(ang, s_tok, t)
            TM.put(kf, c_tok)
            L = [pc("diff_lambda_2", 64 * i, 64) for i in range(4)]
            for i in range(2):
                buf, free = TM.get()
                t = V.do(lambda e: e.tensor_tensor(buf[:, 0:64], L[2 * i], L[2 * i + 1], ALU.mult), free, t_par)
                t = V.do(lambda e, i=i: e.tensor_reduce(lamb[:, i:i + 1], buf[:, 0:64], AX.X, ALU.add), t)
                TM.put(buf, t)
            t = A.do(lambda e: e.activation(lamb[:, 2:4], lamb[:, 0:2], ACT.Exp), t)
            t = V.do(lambda e: e.tensor_tensor(lamb[:, 4:5], lamb[:, 3:4], lamb[:, 2:3], ALU.subtract), t)
            t = V.do(lambda e: e.tensor_scalar(lamb[:, 4:5], lamb[:, 4:5], LAMBDA_INIT, None, ALU.subtract), t)
            lam_tok = V.do(lambda e: e.tensor_scalar(lamb[:, 5:6], pc("diff_subln_g_2"), 1.0 - LAMBDA_INIT, None,
                                                     ALU.mult), t)

            v_tok = []
            for half in range(2):
                def keep_dv(j, bank, t):
                    v_tok.append(A.do(lambda e: e.activation(vals[:, j, 512 * half:512 * half + 512], bank, ACT.Copy),
                                      t, ph))
                    PS.put(bank, v_tok[-1])
                linear_tokens("dv", yhi, ylo, ytok, keep_dv)

            def rotated(dst):
                bank, t = linear("dqk", yhi, ylo, ytok)
                x, xf = TM.get()
                t = A.do(lambda e: e.activation(x[:, 0:S], bank, ACT.Copy), t, xf)
                PS.put(bank, t)
                bank, free = PS.get()
                mm = T.do(lambda e: e.matmul(bank, cst[:, PERM:PERM + 128], x[:, 0:S], start=True, stop=True), t, free)
                a = V.do(lambda e: e.tensor_tensor(dst, bank, sinr[:, :], ALU.mult), mm, s_tok, ph)
                PS.put(bank, a)
                b = G.do(lambda e: e.tensor_tensor(x[:, 0:S], x[:, 0:S], cosr[:, :], ALU.mult), mm, c_tok)
                t = G.do(lambda e: e.tensor_tensor(dst, dst, x[:, 0:S], ALU.add), a, b)
                TM.put(x, t)
                return t

            p_free = [None, None]
            a_free = [None, None]
            o_tok = []
            turn = [0]

            def softmaxes(h, i, q_tok, k_tok):
                n = turn[0] % 2
                turn[0] += 1
                wd = 128 * (i + 1)
                got = [PS.get() for _ in range(2)]
                m = sm[:, n, :]
                mx = []
                for c in range(2):
                    bank, free = got[c]
                    rows = slice(64 * c, 64 * c + 64)
                    mm = T.do(lambda e, bank=bank, rows=rows: e.matmul(
                        bank[:, 0:wd], qs[rows, h, 128 * i:128 * i + 128], ks[rows, h, 0:wd], start=True, stop=True),
                        q_tok, k_tok, free)
                    d = bank[:, 128 * i:wd]
                    t = V.do(lambda e, d=d: e.tensor_tensor(d, d, cst[:, CNEG:CNEG + 128], ALU.add), mm)
                    t = V.do(lambda e, bank=bank, c=c: e.tensor_reduce(m[:, c:c + 1], bank[:, 0:wd], AX.X, ALU.max),
                             t, p_free[n])
                    mx.append(t)
                t = V.do(lambda e: e.tensor_scalar(m[:, 2:4], m[:, 0:2], -0.125, None, ALU.mult), mx)
                ex = []
                for c in range(2):
                    bank = got[c][0]
                    ex.append(A.do(lambda e, bank=bank, c=c: e.activation(
                        pp[:, n, c, 0:wd], bank[:, 0:wd], ACT.Exp, bias=m[:, 2 + c:3 + c], scale=0.125,
                        accum_out=m[:, 4 + c:5 + c]), t, ph, p_free[n]))
                    PS.put(bank, ex[-1])
                t = V.do(lambda e: e.reciprocal(m[:, 6:8], m[:, 4:6]), ex)
                t = V.do(lambda e: e.tensor_tensor(m[:, 7:8], m[:, 7:8], lamb[:, 4:5], ALU.mult), t, lam_tok)
                t1 = V.do(lambda e: e.tensor_scalar(pp[:, n, 1, 0:wd], pp[:, n, 1, 0:wd], m[:, 7:8], None, ALU.mult), t)
                t = V.do(lambda e: e.scalar_tensor_tensor(pp[:, n, 0, 0:wd], pp[:, n, 0, 0:wd], m[:, 6:7],
                                                          pp[:, n, 1, 0:wd], ALU.mult, ALU.add), t1)
                return n, t

            def values(h, i, n, tok, obank):
                wd = 128 * (i + 1)
                bank, free = PS.get()
                T.wait(free, tok)
                for j in range(i + 1):
                    c = slice(128 * j, 128 * j + 128)
                    mm = (T.do if j == i else T.quiet)(lambda e, c=c: e.transpose(bank[:, c], pp[:, n, 0, c], ident))
                p_free[n] = mm
                t = A.do(lambda e: e.activation(aT[:, n, 0:wd], bank[:, 0:wd], ACT.Copy), mm, a_free[n], ph)
                PS.put(bank, t)
                for j in range(i + 1):
                    mm = (T.do if j == i else T.quiet)(lambda e, j=j: e.matmul(
                        obank[:, 128 * i:128 * i + 128], vals[:, j, 128 * h:128 * h + 128],
                        aT[:, n, 128 * j:128 * j + 128], start=j == 0, stop=j == i), t, v_tok)
                a_free[n] = mm
                return mm

            prev = None
            nxt_qk = (rotated(qs[:, 0, :]), rotated(ks[:, 0, :]))
            for h in range(8):
                q_tok, k_tok = nxt_qk
                obank, ofree = PS.get()
                T.wait(ofree)
                pend = []
                for i in range(4):
                    pend.append((i, *softmaxes(h, i, q_tok, k_tok)))
                    if i == 1 and h < 7:
                        a = rotated(qs[:, h + 1, :])
                    if i == 3 and h < 7:
                        nxt_qk = (a, rotated(ks[:, h + 1, :]))
                    if len(pend) > 1:
                        i0, n0, t0 = pend.pop(0)
                        values(h, i0, n0, t0, obank)
                i0, n0, t0 = pend.pop(0)
                mm = values(h, i0, n0, t0, obank)
                o_tok.append(A.do(lambda e: e.activation(qs[:, h, :], obank, ACT.Copy), mm))
                PS.put(obank, o_tok[-1])
            y_read = T.last()
            bank, free = PS.get()
            for h in range(8):
                buf, t = square(qs[:, h, :], o_tok[h])
                mm = add_columns(bank, 4 * h, buf, h == 0, h == 7, t, free)
                TM.put(buf, mm)
            r_tok = root(bank, 32, mm, 1.0 / 128)
            x_tok = []
            for h in range(8):
                R, t = spread(4 * h, r_tok)
                buf, free = TM.get()
                t = V.do(lambda e: e.scalar_tensor_tensor(buf[:, 0:S], qs[:, h, :], lamb[:, 5:6], R,
                                                          ALU.mult, ALU.mult), t, free, lam_tok, o_tok[h])
                PS.put(R, t)
                x_tok.append(split(yhi[:, h, :], ylo[:, h, :], buf[:, 0:S], t, y_read))
                TM.put(buf, x_tok[-1])
            result = add_gated(17)
            for n in range(NT):
                bank, t = linear("do", yhi, ylo, x_tok)
                PS.put(bank, result(0, n, bank, t))
            y_free[0] = T.last()
        phase_end()

        ytok = prenorm(pc("norm_g_2", 24, 8), 18, 19)
        ffn("mlp1", ytok, [8] * 4, False, add_gated(20))

        R, r_tok = rms([h_sb[:, n, :] for n in range(NT)], htok)
        for n in range(NT):
            buf, free = TM.get()
            t = V.do(lambda e, n=n, buf=buf: e.scalar_tensor_tensor(
                buf[:, 0:S], h_sb[:, n, :], pc("final_g_2", n), R, ALU.mult, ALU.mult), r_tok, free, htok[n])
            Y.dma(lambda e, n=n, buf=buf: e.dma_start(out[n], buf[:, 0:S]), (s_out[n], 16), t)
            TM.put(buf, (s_out[n], 16))
        assert state["at"] == len(stream) and not state["prepped"]
        block = ctx.enter_context(nc.Block())

        @block.sync
        def _(e):
            for n in range(NT):
                e.wait_ge(s_out[n], 16)


def by_feature(w):
    k, n = w.shape
    return w.reshape(k // 128, 128, n // 128, 128).transpose(2, 1, 0, 3).reshape(n // 128, 128, k)


def by_rows(w):
    n = w.shape[1] // 512
    return w.reshape(4, 2, 128, n, 512).transpose(3, 0, 2, 1, 4).reshape(4 * n, 128, 1024)


def lay_out(x):
    d = {}
    offs, n_par = param_offsets()
    par = np.zeros((128, n_par), np.float32)
    for name, n in PARAMS:
        a = x[name].reshape(-1)
        if name == "mlstm_gate_b":
            par[0:8, offs[name]] = a
        elif name == "diff_lambda_2":
            par[:, offs[name]:offs[name] + n] = a[None, :]
        else:
            par[:, offs[name]:offs[name] + n] = a.reshape(n, 128).T
    d["par"] = par
    d["cst"], d["msk"] = constants()
    d["x"] = x["x"][0].T.reshape(8, 128, S).transpose(1, 0, 2)
    d["pos"] = np.broadcast_to(x["positions_2"].reshape(1, S), (128, S))
    d["a2"] = x["gla_w_a2_2"][0]
    d["ada"] = x["ada_w"][0].reshape(8, 128, 9, 1024).transpose(2, 0, 1, 3)
    d["ada_2"] = x["ada_w_2"].reshape(2, 8, 128, 6, 1024).transpose(0, 3, 1, 2, 4).reshape(12, 8, 128, 1024)
    for b in ("ffn1", "ffn2"):
        gate, up, down = (x[f"{b}_w_{p}"][0] for p in ("gate", "up", "down"))
        for g in range(3):
            c = slice(1024 * g, min(F1, 1024 * g + 1024))
            a, u = by_feature(gate[:, c]), by_feature(up[:, c])
            d[f"{b}_up{g}"] = np.stack([a, u], 1).reshape(-1, 128, 1024)
            d[f"{b}_dn{g}"] = by_feature(down[c])
    w = x["w_in"][0]
    d["w_mqk"] = by_feature(w[:, 0:1024])
    d["w_mif"] = by_feature(w[:, 2048:2176])
    d["w_mv"] = by_rows(w[:, 1024:1536])
    d["w_mo"] = by_feature(w[:, 1536:2048])
    d["w_hq"] = by_feature(w[:, 2056:2568])
    d["w_hf"] = by_feature(w[:, 2568:3080])
    d["w_hi"] = by_rows(w[:, 3080:3592])
    d["w_hg"] = by_feature(w[:, 3592:4104])
    d["w_wout"] = by_feature(x["w_out"][0])
    w = x["gla_w_in_2"][0]
    d["w_gq"] = by_feature(w[:, 0:512])
    d["w_gk"] = by_feature(w[:, 512:1024])
    d["w_gv"] = by_rows(w[:, 1024:2048])
    d["w_gr"] = by_feature(w[:, 2048:3072])
    d["w_ga"] = by_feature(np.concatenate([w[:, 3072:3088], w[:, 0:112]], 1))
    d["w_go"] = by_feature(x["gla_w_o_2"][0])
    w = x["diff_w_in_2"][0]
    q, k = by_feature(w[:, 0:1024]), by_feature(w[:, 1024:2048])
    d["w_dqk"] = np.stack([q, k], 1).reshape(16, 128, 1024)
    d["w_dv"] = by_rows(w[:, 2048:3072])
    d["w_do"] = by_feature(x["diff_w_o_2"][0])
    for layer in range(2):
        w1, w2 = x["mlp_w1_2"][layer], x["mlp_w2_2"][layer]
        for g in range(4):
            c = slice(1024 * g, 1024 * g + 1024)
            d[f"mlp{layer}_up{g}"] = by_feature(w1[:, c])
            d[f"mlp{layer}_dn{g}"] = by_feature(w2[c])
    return {k: np.ascontiguousarray(v) for k, v in d.items()}


def kernel(**inputs):
    import concourse.bacc as bacc
    from concourse.bass_utils import run_bass_kernel_spmd

    arrays = lay_out({k: np.asarray(v) for k, v in inputs.items()})
    nc = bacc.Bacc("TRN2", target_bir_lowering=False, num_devices=1)
    dram, feed = {}, {}
    for name, a in arrays.items():
        feed[f"in_{name}"] = a
        dram[name] = nc.dram_tensor(f"in_{name}", a.shape, mybir.dt.from_np(a.dtype), kind="ExternalInput").ap()
    out = nc.dram_tensor("out_y", (NT, 128, S), mybir.dt.float32, kind="ExternalOutput").ap()
    build_program(nc, dram, out)
    got = run_bass_kernel_spmd(nc, [feed], core_ids=[0]).results[0]["out_y"]
    return np.ascontiguousarray(np.asarray(got).reshape(D, S).T).reshape(1, S, D)
```

```python
import math
from collections import deque
from contextlib import ExitStack

import numpy as np

import concourse.bass as bass
from concourse import mybir

S = 512
D = 1024
NT = D // 128
EPS = 1e-6
NRAW = 6
NW = 3
NTMP = 8
FFN_GROUPS = (8, 6, 8)
NACC = 3
ADA_PLAN = [((2, 4, 3, 5, 7, 6), None, "ffn1_up2"), ((8, 10, 9, 11, 13, 12), "ffn2_up0", "ffn2_up2"),
            ((14, 16, 15, 17, 19, 18), "mlp0_up0", "mlp0_up3"), ((20,), "mlp1_up0", "mlp1_up1")]
BIG = 1e30
LAMBDA_INIT = 0.8 - 0.6 * math.exp(-0.3)
MAGIC = 12582912.0
PI_A, PI_B, PI_C = 6.28125, 2029 / 2**20, 2 * math.pi - 6.28125 - 2029 / 2**20
INV_FREQ = np.power(np.float32(500000.0), -np.arange(0, 16, 2, dtype=np.float32) / np.float32(16)).astype(np.float32)

PARAMS = [
    ("c", 8), ("c_2", 8), ("ada_b", 72), ("ada_b_2", 96), ("ffn1_pre_g", 8), ("ffn1_post_g", 8),
    ("mix_pre_g", 8), ("mix_post_g", 8), ("mlstm_conv_w", 32), ("mlstm_conv_b", 8),
    ("mlstm_norm_g", 4), ("hgrn_lb_logits", 8), ("hgrn_norm_g", 4), ("ffn2_pre_g", 8),
    ("ffn2_post_g", 8), ("norm_g_2", 32), ("gla_b_a_2", 4), ("gla_b_r_2", 8), ("gla_norm_g_2", 2),
    ("diff_subln_g_2", 1), ("final_g_2", 8), ("mlstm_gate_b", 1), ("diff_lambda_2", 256),
]
IDENT, ONES, PERM, CAUS, CNEG, INVF_C, EPS_C, HPI_C, SEL_C, SEL_R, SEL_M, NCONST = \
    0, 128, 256, 384, 512, 640, 641, 642, 643, 647, 678, 742
MIX_ORDER = [("mif", 0, 1), ("hq", 0, 4), ("hf", 0, 4), ("hi", 0, 4)]
MIX_ORDER += [("mqk", i, i + 1) for i in (0, 4, 1, 5, 2, 6, 3, 7)]
MIX_ORDER += [("mv", 0, 4), ("hg", 0, 4), ("mo", 0, 4), ("wout", 0, 8)]
LEVELS = [1, 2, 4, 8, 16, 32, 64]


def param_offsets():
    at, out = 0, {}
    for name, n in PARAMS:
        out[name] = at
        at += n
    return out, at


def constants():
    c = np.zeros((128, NCONST), np.float32)
    i = np.arange(128)
    c[:, IDENT:IDENT + 128] = np.eye(128)
    c[:, ONES:ONES + 128] = 1.0
    for g in (0, 64):
        for d in range(8):
            c[g + d + 8, PERM + g + d] = -1.0
            c[g + d, PERM + g + d + 8] = 1.0
            c[g + d, INVF_C] = c[g + d + 8, INVF_C] = INV_FREQ[d]
    c[:, CAUS:CAUS + 128] = np.where(i[None, :] < i[:, None], BIG, 0.0)
    c[:, CNEG:CNEG + 128] = np.where(i[None, :] > i[:, None], -BIG, 0.0)
    c[:, EPS_C] = EPS
    c[:, HPI_C] = math.pi / 2
    for h in range(4):
        c[4 + h, SEL_C + h] = 1.0
        for j in range(4):
            c[h, SEL_M + 16 * j + 4 * h + j] = 1.0
    c[:, SEL_R + 15] = 1.0
    m = np.zeros((128, 7, 128), np.float32)
    for n, h in enumerate(LEVELS):
        s, t = i[:, None], i[None, :]
        m[:, n, :] = (s // (2 * h) == t // (2 * h)) & (s % (2 * h) < h) & (t % (2 * h) >= h)
    return c, m.reshape(128, 896)


class Queue:

    def __init__(self, engine, sem):
        self.engine, self.sem, self.n, self.seen = engine, sem, 0, {}

    def wait(self, *tokens):
        for t in tokens:
            if t is None:
                continue
            if isinstance(t, list):
                self.wait(*t)
                continue
            sem, value = t
            if self.seen.get(sem.name, 0) < value:
                self.seen[sem.name] = value
                self.engine.wait_ge(sem, value)

    def quiet(self, fn, *tokens):
        self.wait(*tokens)
        fn(self.engine)

    def do(self, fn, *tokens):
        self.wait(*tokens)
        self.n += 1
        fn(self.engine).then_inc(self.sem, 1)
        return (self.sem, self.n)

    def last(self):
        return (self.sem, self.n) if self.n else None

    def dma(self, fn, token, *tokens):
        self.wait(*tokens)
        fn(self.engine).then_inc(token[0], 16)
        return token


class Buffers:

    def __init__(self, views):
        self.free = deque((v, None) for v in views)

    def get(self):
        return self.free.popleft()

    def put(self, view, *tokens):
        self.free.append((view, list(tokens)))


def build_program(nc, dram, out):
    fp32, f32r, u8, i32 = mybir.dt.float32, mybir.dt.float32r, mybir.dt.uint8, mybir.dt.int32
    ALU, ACT, AX = mybir.AluOpType, mybir.ActivationFunctionType, mybir.AxisListType
    offs, NP = param_offsets()
    ctx = ExitStack()
    with ctx:
        def sb(name, shape, dt=fp32, stack=ctx):
            return stack.enter_context(nc.sbuf_tensor(name, shape, dt))

        def sem(name):
            return ctx.enter_context(nc.semaphore(name))

        h_sb = sb("h_sb", [128, NT, S])
        yhi = sb("yhi", [128, NT, S], f32r)
        ylo = sb("ylo", [128, NT, S], f32r)
        raw = sb("raw", [128, NRAW, 1024])
        whi = sb("whi", [128, NW, 1024], f32r)
        wlo = sb("wlo", [128, NW, 1024], f32r)
        cst = sb("cst", [128, NCONST])
        msk = sb("msk", [128, 7, 128], u8)
        par = sb("par", [128, NP])
        mod = sb("mod", [128, 168])
        acc2 = sb("acc", [128, NACC, 1024])
        sil = sb("sil", [128, 16])
        coef = sb("coef", [128, 32])
        stat = sb("stat", [128, 17])
        lbc = sb("lbc", [128, 8, 4])
        lamb = sb("lamb", [128, 8])
        tmps = sb("tmps", [128, NTMP, 516])
        banks = [ctx.enter_context(nc.psum_tensor(f"bank{i}", [128, S], fp32)) for i in range(8)]

        T, A, V, G, Y = (Queue(e, sem(f"s_{n}")) for e, n in (
            (nc.tensor, "pe"), (nc.scalar, "act"), (nc.vector, "dve"), (nc.gpsimd, "pool"), (nc.sync, "sp")))
        s_raw = [sem(f"s_raw{i}") for i in range(NRAW)]
        s_par, s_cst, s_x, s_msk = sem("s_par"), sem("s_cst"), sem("s_x"), sem("s_msk")
        s_out = [sem(f"s_out{n}") for n in range(NT)]
        PS = Buffers([b[:, :] for b in banks])
        TM = Buffers([tmps[:, i, :] for i in range(NTMP)])

        ident = cst[:, IDENT:IDENT + 128]
        ones = cst[:, ONES:ONES + 128]
        one = cst[:, ONES:ONES + 1]
        eps = cst[:, EPS_C:EPS_C + 1]

        def pc(name, i=0, n=1, p=128):
            return par[0:p, offs[name] + i:offs[name] + i + n]

        def f(ap):
            return ap.bitcast(fp32)

        def bc(ap, n, axis):
            v = ap.unsqueeze(axis)
            shape = list(v.shape)
            shape[axis] = n
            return v.to_broadcast(shape)

        t_par = Y.dma(lambda e: e.dma_start(par[:, :], dram["par"]), (s_par, 16))
        t_cst = Y.dma(lambda e: e.dma_start(cst[:, :], dram["cst"]), (s_cst, 16))
        last_acc = acc2[:, NACC - 1, 0:896]
        t_msk = Y.dma(lambda e: e.dma_start(last_acc, dram["msk"]), (s_msk, 16))
        t_msk = V.do(lambda e: e.tensor_copy(msk[:, :, :].rearrange("p n t -> p (n t)"), last_acc), t_msk)
        t_x = A.dma(lambda e: e.dma_start(h_sb[:, :, :], dram["x"]), (s_x, 16))
        t_sil = A.do(lambda e: e.activation(sil[:, 0:16], pc("c", 0, 16), ACT.Silu), t_par)

        lin, ada = [], {}

        marks = {}

        def add_units(name, tag, i0, i1, width=1024):
            for i in range(i0, i1):
                lin.append((name, i, tag, width))
                marks[tag] = len(lin)

        def add(name, tag, width=1024):
            add_units(name, tag, 0, dram[name].shape[0], width)

        for b, n in (("ffn1", 3), ("mix", 0), ("ffn2", 3)):
            if b == "mix":
                for part in MIX_ORDER:
                    add_units("w_" + part[0], part[0], part[1], part[2])
                continue
            ups = FFN_GROUPS
            for g in range(n):
                add(f"{b}_up{g}", f"{b}_up{g}")
                if g:
                    add(f"{b}_dn{g - 1}", f"{b}_dn{g - 1}", 128 * ups[g - 1])
            add(f"{b}_dn{n - 1}", f"{b}_dn{n - 1}", 128 * ups[n - 1])
        for layer in range(2):
            if layer == 0:
                for part in ("ga", "gq", "gk", "gv", "gr", "go"):
                    add("w_" + part, part)
            else:
                add_units("w_dqk", "dqk", 0, 3)
                add("w_dv", "dv")
                add_units("w_dqk", "dqk", 3, 16)
                add("w_do", "do")
            b = f"mlp{layer}"
            for g in range(4):
                add(f"{b}_up{g}", f"{b}_up{g}")
                if g:
                    add(f"{b}_dn{g - 1}", f"{b}_dn{g - 1}")
            add(f"{b}_dn3", f"{b}_dn3")
        stream = [("ada", (v, kt)) for v in (1, 0) for kt in range(8)]
        for vs, start, end in ADA_PLAN:
            todo = [(v, kt) for v in vs for kt in range(8)]
            a, b = marks[start] if start else 0, marks[end]
            for n, x in enumerate(todo):
                ada.setdefault(a + n * (b - a) // len(todo), []).append(x)
        for n, u in enumerate(lin):
            stream.append(("lin", u))
            stream += [("ada", x) for x in ada.get(n, [])]
        state = {"at": 0, "lin": 0, "prepped": deque(), "acc": None, "acc_read": [None] * (NACC - 1) + [t_msk], "vec": 0}
        raw_free = [None] * NRAW
        w_free = [None] * NW
        mod_tok = [None] * 21
        summed, columns = deque(), {}

        def mod_columns():
            v, acc, b, t = summed.popleft()
            bank, free = PS.get()
            for j in range(8):
                mm = (T.do if j == 7 else T.quiet)(
                    lambda e, j=j: e.matmul(bank[:, j:j + 1], acc[:, 128 * j:128 * j + 128], one,
                                            start=True, stop=True), t, free, t_cst)
            state["acc_read"][b] = mm
            columns[v] = bank, mm

        def mod_bias(v):
            bank, mm = columns.pop(v)
            bias = pc("ada_b", 8 * v, 8) if v < 9 else pc("ada_b_2", 8 * (v - 9), 8)
            mod_tok[v] = V.do(lambda e: e.tensor_tensor(mod[:, 8 * v:8 * v + 8], bank[:, 0:8], bias,
                                                        ALU.add), mm, t_par)
            PS.put(bank, mod_tok[v])

        def known(v):
            return mod_tok[v] is not None or v in columns or any(x[0] == v for x in summed)

        def mod_column(v):
            while mod_tok[v] is None and v not in columns:
                if any(x[0] == v for x in summed):
                    mod_columns()
                else:
                    pump_one()

        def mods_bias():
            for v in list(columns):
                mod_bias(v)

        def pump_one():
            n = state["at"]
            state["at"] += 1
            kind, u = stream[n]
            slot = n % NRAW
            token = (s_raw[slot], 16 * (n // NRAW + 1))
            if kind == "ada":
                v, kt = u
                src = dram["ada"][v, kt] if v < 9 else dram["ada_2"][v - 9, kt]
                Y.dma(lambda e: e.dma_start(raw[:, slot, :], src), token, raw_free[slot])
                b = state["vec"] % NACC
                acc = acc2[:, b, :]
                col = sil[:, kt:kt + 1] if v < 9 else sil[:, 8 + kt:9 + kt]
                if kt == 0:
                    if len(summed) == NACC:
                        mod_columns()
                        mods_bias()
                    t = V.do(lambda e: e.tensor_scalar(acc, raw[:, slot, :], col, None, ALU.mult),
                             token, t_sil, state["acc_read"][b])
                else:
                    t = V.do(lambda e: e.scalar_tensor_tensor(acc, raw[:, slot, :], col, acc,
                                                              ALU.mult, ALU.add), token, state["acc"])
                state["acc"] = raw_free[slot] = t
                if kt == 7:
                    summed.append((v, acc, b, t))
                    state["vec"] += 1
                return
            name, i, tag, width = u
            src = dram[name][i]
            Y.dma(lambda e: e.dma_start(raw[:, slot, 0:width], src), token, raw_free[slot])
            w = state["lin"] % NW
            state["lin"] += 1
            hi = A.do(lambda e: e.activation(whi[:, w, 0:width], raw[:, slot, 0:width], ACT.Copy),
                      token, w_free[w])
            lo = V.do(lambda e: e.tensor_tensor(wlo[:, w, 0:width], raw[:, slot, 0:width],
                                                f(whi[:, w, 0:width]), ALU.subtract), hi, w_free[w])
            raw_free[slot] = lo
            state["prepped"].append((tag, w, [hi, lo]))

        def pump(ahead):
            while len(state["prepped"]) < ahead and state["at"] < len(stream):
                pump_one()

        def need_mod(v):
            mod_column(v)
            if mod_tok[v] is None:
                mod_bias(v)
            return mod_tok[v]

        def need_mods(*vs):
            for v in vs:
                mod_column(v)
            for v in vs:
                need_mod(v)

        def unit(tag):
            pump(NW - 1)
            got, w, toks = state["prepped"].popleft()
            assert got == tag, (got, tag)
            return w, toks

        def used(w, tok):
            w_free[w] = tok
            pump(NW - 1)

        def linear(tag, xh, xl, xtoks, order=None):
            w, toks = unit(tag)
            bank, free = PS.get()
            kts = len(xtoks)
            order = order or list(range(kts))
            T.wait(free, toks)
            for kt in order:
                wh, wl = whi[:, w, 128 * kt:128 * kt + 128], wlo[:, w, 128 * kt:128 * kt + 128]
                a, b = xh[:, kt, :], xl[:, kt, :]
                first, last = kt == order[0], kt == order[-1]
                T.quiet(lambda e: e.matmul(bank, wh, a, start=first, stop=False), xtoks[kt])
                T.quiet(lambda e: e.matmul(bank, wh, b, start=False, stop=False))
                mm = (T.do if last else T.quiet)(lambda e: e.matmul(bank, wl, a, start=False, stop=last))
            used(w, mm)
            return bank, mm

        def linear_halves(tag, xh, xl, xtoks):
            w, toks = unit(tag)
            bank, free = PS.get()
            T.wait(free, toks)
            for kt in range(8):
                if kt == 4:
                    yield None
                wh, wl = whi[:, w, 128 * kt:128 * kt + 128], wlo[:, w, 128 * kt:128 * kt + 128]
                a, b = xh[:, kt, :], xl[:, kt, :]
                T.quiet(lambda e: e.matmul(bank, wh, a, start=kt == 0, stop=False), xtoks[kt])
                T.quiet(lambda e: e.matmul(bank, wh, b, start=False, stop=False))
                mm = (T.do if kt == 7 else T.quiet)(lambda e: e.matmul(bank, wl, a, start=False, stop=kt == 7))
            used(w, mm)
            yield bank, mm

        def linear_pair(tags, xh, xl, xtoks, order=None, hooks={}):
            units = [unit(tag) for tag in tags]
            got = [PS.get() for _ in tags]
            order = order or list(range(len(xtoks)))
            for kt in order:
                if kt in hooks:
                    hooks[kt]()
                for (w, toks), (bank, free) in zip(units, got):
                    wh, wl = whi[:, w, 128 * kt:128 * kt + 128], wlo[:, w, 128 * kt:128 * kt + 128]
                    a, first = xh[:, kt, :], kt == order[0]
                    T.quiet(lambda e: e.matmul(bank, wh, a, start=first, stop=False), xtoks[kt][0], free, toks)
                    T.quiet(lambda e: e.matmul(bank, wl, a, start=False, stop=False))
            out = []
            for (w, _), (bank, _) in zip(units, got):
                for kt in order:
                    wh, b = whi[:, w, 128 * kt:128 * kt + 128], xl[:, kt, :]
                    last = kt == order[-1]
                    mm = (T.do if last else T.quiet)(
                        lambda e: e.matmul(bank, wh, b, start=False, stop=last), xtoks[kt][1])
                used(w, mm)
                out.append((bank, mm))
            return out

        def linear_tokens(tag, xh, xl, xtoks, evac):
            got = [PS.get() for _ in range(4)]
            for kp in range(4):
                w, toks = unit(tag)
                for j in range(4):
                    bank, free = got[j]
                    T.wait(free, toks)
                    for k2 in range(2):
                        kt = 2 * kp + k2
                        wh, wl = whi[:, w, 512 * k2:512 * k2 + 512], wlo[:, w, 512 * k2:512 * k2 + 512]
                        a, b = xh[:, kt, 128 * j:128 * j + 128], xl[:, kt, 128 * j:128 * j + 128]
                        first, last = kt == 0, kt == 7
                        T.quiet(lambda e, bank=bank, wh=wh, a=a, first=first:
                                e.matmul(bank, a, wh, start=first, stop=False), xtoks[kt])
                        T.quiet(lambda e, bank=bank, wh=wh, b=b: e.matmul(bank, b, wh, start=False, stop=False))
                        mm = (T.do if k2 == 1 else T.quiet)(
                            lambda e, bank=bank, wl=wl, a=a, last=last: e.matmul(bank, a, wl, start=False, stop=last))
                    if kp == 3:
                        evac(j, bank, mm)
                used(w, mm)

        def square(src, tok):
            buf, free = TM.get()
            t = A.do(lambda e: e.activation(buf[:, 0:S], src, ACT.Square), tok, free)
            return buf, t

        def to_row(r):
            return cst[:, SEL_R + 15 - r:SEL_R + 31 - r]

        def add_rows(bank, row, buf, first, last, *toks):
            for j in range(4):
                mm = (T.do if j == 3 else T.quiet)(
                    lambda e, j=j: e.matmul(bank[0:16, 0:128], to_row(row + j), buf[:, 128 * j:128 * j + 128],
                                            start=first and j == 0, stop=last and j == 3), *toks)
            return mm

        def ready_root():
            state["warm"] = A.do(lambda e: e.activation(stat[:, 16:17], eps, ACT.Sqrt), t_cst, state.get("warm"))

        def root(bank, tok, scale):
            buf, free = TM.get()
            t = A.do(lambda e: e.activation(buf[0:16, 0:128], bank[0:16, 0:128], ACT.Sqrt, bias=eps[0:16], scale=scale),
                     tok, free)
            PS.put(bank, t)
            return buf, V.do(lambda e: e.reciprocal(buf[0:16, 0:128], buf[0:16, 0:128]), t)

        def spread(rows, row, n=16):
            buf, tok = rows
            bank, free = PS.get()
            for j in range(4):
                mm = (T.do if j == 3 else T.quiet)(
                    lambda e: e.matmul(bank[:, 128 * j:128 * j + 128],
                                       cst[0:n, IDENT + row + j:IDENT + row + j + 1].to_broadcast([n, 128]),
                                       buf[0:n, 0:128], start=True, stop=True), tok, free)
            return bank, mm

        def warm(n):
            bank, free = PS.get()
            for i in range(n):
                mm = (T.do if i == n - 1 else T.quiet)(
                    lambda e: e.matmul(bank, ones, cst[:, 0:S], start=True, stop=True), free, t_cst)
            PS.put(bank, mm)

        class Sums:

            def __init__(self):
                self.bank = self.sum = None

            def total(self, buf, last, *toks):
                first = self.bank is None
                if first:
                    self.bank, self.free = PS.get()
                for j in range(4):
                    self.mm = (T.do if j == 3 else T.quiet)(
                        lambda e: e.matmul(self.bank[0:4, 0:128], cst[:, SEL_R + 15 - j:SEL_R + 19 - j],
                                           buf[:, 128 * j:128 * j + 128], start=first and j == 0,
                                           stop=last and j == 3), self.free, t_cst, *toks)
                TM.put(buf, self.mm)

            def add(self, src, tok, last, direct=False):
                if last:
                    ready_root()
                buf, t = square(src, tok)
                if last and self.sum is not None:
                    self.total(self.sum, False, self.tok)
                if last and not direct:
                    warm(1)
                if last or direct:
                    self.total(buf, last, t)
                elif self.sum is None:
                    self.sum, self.tok = buf, t
                else:
                    total = self.sum
                    self.tok = G.do(lambda e: e.tensor_tensor(total[:, 0:S], total[:, 0:S], buf[:, 0:S], ALU.add),
                                    t, self.tok)
                    TM.put(buf, self.tok)

            def root(self, v):
                buf, free = TM.get()
                t = A.do(lambda e: e.activation(buf[0:4, 0:128], self.bank[0:4, 0:128], ACT.Sqrt, bias=eps[0:4],
                                                scale=1.0 / D), self.mm, free)
                PS.put(self.bank, t)
                t = V.do(lambda e: e.reciprocal(buf[0:4, 0:128], buf[0:4, 0:128]), t)
                if v is not None:
                    mod_column(v)
                    warm(2)
                bank, mm = spread((buf, t), 0, 4)
                TM.put(buf, mm)
                if v is not None:
                    warm(2)
                return bank, mm

        htok = [t_x] * NT
        h_read = [None] * NT
        y_free = [None]

        def split(dst_hi, dst_lo, src, tok, *free):
            hi = A.do(lambda e: e.activation(dst_hi, src, ACT.Copy), tok, *free)
            lo = V.do(lambda e: e.tensor_tensor(dst_lo, src, f(dst_hi), ALU.subtract), hi, *free)
            return [hi, lo]

        def to_y(items, free):
            his = [A.do(lambda e: e.activation(yhi[:, n, :], src, ACT.Copy), tok, free) for n, src, tok in items]
            return [[hi, V.do(lambda e: e.tensor_tensor(ylo[:, n, :], src, f(yhi[:, n, :]), ALU.subtract), hi, free)]
                    for (n, src, _), hi in zip(items, his)]

        def prenorm(g, v_shift, v_scale, sums):
            A_c = coef[:, 0:8]
            if state["lin"]:
                pump(NW)
            R, r_tok = sums.root(v_scale if state["lin"] else None)
            c_tok = V.do(lambda e: e.scalar_tensor_tensor(A_c, mod[:, 8 * v_scale:8 * v_scale + 8], 1.0, g,
                                                          ALU.add, ALU.mult),
                         need_mod(v_scale), t_par, state.get("coef_read"))
            ytok, pend, early = [], deque(), deque()

            def scaled(n):
                buf, free = TM.get()
                h_read[n] = V.do(lambda e: e.scalar_tensor_tensor(
                    buf[:, 0:S], h_sb[:, n, :], A_c[:, n:n + 1], R, ALU.mult, ALU.mult),
                    c_tok, r_tok, free, htok[n], y_free[0])
                return buf, h_read[n]

            if not known(v_shift):
                warm(3)
            while not known(v_shift):
                pump_one()
                if not known(v_shift):
                    pump_one()
                early.append(scaled(len(early)))
            mod_column(v_shift)
            pump(NW - 1)

            def low(n, buf, hi):
                sh = mod[:, 8 * v_shift + n:8 * v_shift + n + 1]
                lo = V.do(lambda e: e.scalar_tensor_tensor(ylo[:, n, :], buf[:, 0:S], sh, f(yhi[:, n, :]),
                                                           ALU.add, ALU.subtract), hi)
                TM.put(buf, lo)
                ytok.append([hi, lo])

            for n in range(NT):
                if len(pend) == NTMP - 1:
                    low(*pend.popleft())
                buf, t = early.popleft() if early else scaled(n)
                need_mod(v_shift)
                sh = mod[:, 8 * v_shift + n:8 * v_shift + n + 1]
                hi = A.do(lambda e: e.activation(yhi[:, n, :], buf[:, 0:S], ACT.Identity, bias=sh),
                          t, y_free[0], mod_tok[v_shift])
                pend.append((n, buf, hi))
            while pend:
                low(*pend.popleft())
            state["coef_read"] = t
            PS.put(R, t)
            return ytok

        def postnorm(tiles, toks, sums, g, v_gate, half):
            C = coef[:, 8:16]
            R, r_tok = sums.root(v_gate)
            c_tok = V.do(lambda e: e.scalar_tensor_tensor(C, mod[:, 8 * v_gate:8 * v_gate + 8], half, g,
                                                          ALU.mult, ALU.mult),
                         need_mod(v_gate), t_par, state.get("coef_read"))
            after = Sums()
            for n in range(NT):
                buf, free = TM.get()
                t = V.do(lambda e: e.scalar_tensor_tensor(
                    buf[:, 0:S], tiles[n], C[:, n:n + 1], R, ALU.mult, ALU.mult), c_tok, r_tok, free, toks[n])
                htok[n] = (V if n in (3, 6, 7) else G).do(
                    lambda e: e.tensor_tensor(h_sb[:, n, :], h_sb[:, n, :], buf[:, 0:S], ALU.add),
                    t, htok[n], h_read[n])
                TM.put(buf, htok[n])
                after.add(h_sb[:, n, :], htok[n], n == NT - 1, direct=True)
            state["coef_read"] = t
            PS.put(R, t)
            return after

        def ffn(name, ytok, counts, gated, result):
            with ExitStack() as st:
                ahi = [sb(f"{name}_ahi{i}", [128, counts[i], S], f32r, st) for i in range(2)]
                alo = [sb(f"{name}_alo{i}", [128, counts[i], S], f32r, st) for i in range(2)]
                a_free = [state.get("phase"), state.get("phase")]
                atok = {}

                first = deque()

                def up(g):
                    nonlocal first
                    toks = []
                    for i in range(counts[g]):
                        tag = f"{name}_up{g}"
                        if (g, i) == (0, 0):
                            first = deque(linear_pair([tag, tag], yhi, ylo, ytok))
                        b1, t1 = first.popleft() if first else linear(tag, yhi, ylo, ytok)
                        buf, free = TM.get()
                        if gated:
                            t = A.do(lambda e: e.activation(buf[:, 0:S], b1, ACT.Silu), t1, free)
                            PS.put(b1, t)
                            b2, t2 = first.popleft() if first else linear(tag, yhi, ylo, ytok)
                            p = V.do(lambda e: e.tensor_tensor(buf[:, 0:S], buf[:, 0:S], b2, ALU.mult), t, t2)
                            PS.put(b2, p)
                        else:
                            t = A.do(lambda e: e.activation(buf[:, 0:S], b1, ACT.Relu), t1, free)
                            PS.put(b1, t)
                            p = V.do(lambda e: e.tensor_tensor(buf[:, 0:S], buf[:, 0:S], buf[:, 0:S], ALU.mult), t)
                        toks.append(split(ahi[g % 2][:, i, :], alo[g % 2][:, i, :], buf[:, 0:S], p, a_free[g % 2]))
                        TM.put(buf, toks[-1])
                    atok[g] = toks
                    y_free[0] = T.last()

                def down(g):
                    for n in range(NT):
                        bank, t = linear(f"{name}_dn{g}", ahi[g % 2], alo[g % 2], atok[g])
                        PS.put(bank, result(g, n, bank, t))
                    a_free[g % 2] = T.last()

                up(0)
                for g in range(1, len(counts)):
                    up(g)
                    down(g - 1)
                down(len(counts) - 1)

        def phase_end():
            state["phase"] = [t for t in (T.last(), A.last(), V.last(), G.last()) if t]

        def gated_ffn(name, ytok, g_post, v_gate, *soon):
            with ExitStack() as st:
                yac = sb(f"{name}_y", [128, NT, S], fp32, st)
                toks = [state.get("phase")] * NT
                sums = Sums()

                def result(g, n, bank, t):
                    if (g, n) == (2, 0):
                        need_mods(v_gate, *soon)
                    if g == 0:
                        toks[n] = A.do(lambda e: e.activation(yac[:, n, :], bank, ACT.Copy), t, toks[n])
                    else:
                        toks[n] = V.do(lambda e: e.tensor_tensor(yac[:, n, :], yac[:, n, :], bank, ALU.add),
                                       t, toks[n])
                    if g == 2:
                        sums.add(yac[:, n, :], toks[n], n == NT - 1)
                    return toks[n]

                ffn(name, ytok, FFN_GROUPS, True, result)
                sums = postnorm([yac[:, n, :] for n in range(NT)], toks, sums, g_post, v_gate, 0.5)
            phase_end()
            return sums

        def add_gated(v_gate, last, *soon):
            sums = Sums()

            def result(g, n, bank, t):
                if (g, n) == (last, 0):
                    need_mods(*soon)
                htok[n] = V.do(lambda e: e.scalar_tensor_tensor(
                    h_sb[:, n, :], bank, mod[:, 8 * v_gate + n:8 * v_gate + n + 1], h_sb[:, n, :],
                    ALU.mult, ALU.add), t, need_mod(v_gate), htok[n], h_read[n])
                if g == last:
                    sums.add(h_sb[:, n, :], htok[n], n == NT - 1)
                return htok[n]
            return result, sums

        def decay_attention(q, k, fd, attd, atto, qt, kt_, ft, masked, bg):
            tt = list(ft)
            ad = [None] * 4
            ao = [[] for _ in range(4)]

            def scores(h):
                bank, free = PS.get()
                for j in range(4):
                    c = slice(128 * j, 128 * j + 128)
                    mm = (T.do if j == 3 else T.quiet)(
                        lambda e, c=c: e.matmul(bank[:, c], k[:, h, c], q[:, h, c], start=True, stop=True),
                        qt[h], kt_[h], free)
                return bank, mm

            def d4(ap):
                return ap.rearrange("p (j t) -> p j t", j=4)

            for h in range(4):
                bank, mm = scores(h)
                ad[h] = V.do(lambda e: e.tensor_tensor(attd[:, h, :, :], d4(bank), bc(ident, 4, 1), ALU.mult),
                             mm, masked)
                PS.put(bank, ad[h])
                qt[h] = V.do(lambda e: e.tensor_tensor(q[:, h, :], q[:, h, :], fd[:, h, 0:S], ALU.mult),
                             mm, qt[h], ft[h])
            bg()
            for n, hh in enumerate(LEVELS + [128, 256]):
                for h in range(4):
                    if hh <= 64:
                        bank, mm = scores(h)
                        ad[h] = V.do(lambda e: e.copy_predicated(attd[:, h, :, :], bc(msk[:, n, :], 4, 1),
                                                                 d4(bank)), mm, ad[h], t_msk)
                        PS.put(bank, ad[h])
                    elif hh == 128:
                        bank, free = PS.get()
                        T.quiet(lambda e: e.matmul(bank[:, 0:128], k[:, h, 0:128], q[:, h, 128:256],
                                                   start=True, stop=True), qt[h], kt_[h], free)
                        mm = T.do(lambda e: e.matmul(bank[:, 128:256], k[:, h, 256:384], q[:, h, 384:512],
                                                     start=True, stop=True))
                        ao[h] += [A.do(lambda e: e.activation(atto[:, h, 0:128], bank[:, 0:128], ACT.Copy),
                                       mm, masked),
                                  A.do(lambda e: e.activation(atto[:, h, 640:768], bank[:, 128:256], ACT.Copy),
                                       mm, masked)]
                        PS.put(bank, ao[h][-1])
                    else:
                        bank, free = PS.get()
                        T.quiet(lambda e: e.matmul(bank[:, 0:256], k[:, h, 0:128], q[:, h, 256:512],
                                                   start=True, stop=True), qt[h], kt_[h], free)
                        mm = T.do(lambda e: e.matmul(bank[:, 256:512], k[:, h, 128:256], q[:, h, 256:512],
                                                     start=True, stop=True))
                        ao[h] += [A.do(lambda e: e.activation(atto[:, h, 128:640], bank, ACT.Copy), mm, masked)]
                        PS.put(bank, ao[h][-1])
                    if hh == 256:
                        continue
                    qv = q[:, h, :].rearrange("p (b x i) -> p b x i", x=2, i=hh)[:, :, 1, :]
                    kv = k[:, h, :].rearrange("p (b x i) -> p b x i", x=2, i=hh)[:, :, 0, :]
                    tv = fd[:, h, :].rearrange("p (b x i) -> p b x i", x=2, i=hh)[:, :, :, 0]
                    t1 = V.do(lambda e: e.tensor_tensor(qv, qv, bc(tv[:, :, 0], hh, 2), ALU.mult),
                              mm, qt[h], tt[h])
                    kt_[h] = G.do(lambda e: e.tensor_tensor(kv, kv, bc(tv[:, :, 1], hh, 2), ALU.mult),
                                  mm, kt_[h], tt[h])
                    qt[h] = t1
                    if hh < 128:
                        tt[h] = V.do(lambda e: e.tensor_tensor(tv[:, :, 0], tv[:, :, 0], tv[:, :, 1], ALU.mult),
                                     tt[h], t1)
                bg()
            return ad, ao

        def mix_values(h, vals, col, attd, atto, toks):
            bank, free = PS.get()
            at = 0
            T.wait(free, toks)
            for j in range(4):
                v = vals[:, j, col:col + 128]
                last = j == 3
                mm = (T.do if last else T.quiet)(
                    lambda e, j=j, v=v, last=last: e.matmul(bank[:, 128 * j:128 * j + 128], v, attd[:, h, j, :],
                                                            start=j == 0, stop=last))
                if not last:
                    w = 384 - 128 * j
                    T.quiet(lambda e, j=j, v=v, at=at, w=w: e.matmul(
                        bank[:, 128 * (j + 1):512], v, atto[:, h, at:at + w], start=False, stop=False))
                    at += w
            return bank, mm

        sums = Sums()
        for n in range(NT):
            sums.add(h_sb[:, n, :], t_x, n == NT - 1, direct=True)
        while state["at"] < 5:
            pump_one()
        ytok = prenorm(pc("ffn1_pre_g", 0, 8), 0, 1, sums)
        sums = gated_ffn("ffn1", ytok, pc("ffn1_post_g", 0, 8), 2, 4, 3)

        ytok = prenorm(pc("mix_pre_g", 0, 8), 3, 4, sums)
        with ExitStack() as st:
            ph = state["phase"]
            mqk = sb("mqk", [128, 8, S], fp32, st)
            vals = sb("vals", [128, 4, S], fp32, st)
            hq = sb("hq", [128, 4, S], fp32, st)
            hf = sb("hf", [128, 4, S], fp32, st)
            hk = sb("hk", [128, 4, S], fp32, st)
            hg = sb("hg", [128, 4, S], fp32, st)
            attd = sb("attd", [128, 4, 4, 128], fp32, st)
            atto = sb("atto", [128, 4, 768], fp32, st)
            mo = hf

            l0, l1 = pc("hgrn_lb_logits", 0, 4), pc("hgrn_lb_logits", 4, 4)
            t = V.do(lambda e: e.tensor_tensor(lbc[:, 0, :], l0, l1, ALU.max), t_par)
            t1 = V.do(lambda e: e.tensor_tensor(lbc[:, 1, :], l0, lbc[:, 0, :], ALU.subtract), t)
            t2 = V.do(lambda e: e.tensor_tensor(lbc[:, 2, :], l1, lbc[:, 0, :], ALU.subtract), t)
            t = A.do(lambda e: e.activation(lbc[:, 3:5, :], lbc[:, 1:3, :], ACT.Exp), t1, t2)
            t = V.do(lambda e: e.tensor_tensor(lbc[:, 5, :], lbc[:, 3, :], lbc[:, 4, :], ALU.add), t)
            t = V.do(lambda e: e.reciprocal(lbc[:, 6, :], lbc[:, 5, :]), t)
            t = V.do(lambda e: e.tensor_tensor(lbc[:, 7, :], lbc[:, 3, :], lbc[:, 6, :], ALU.mult), t)
            lb_tok = V.do(lambda e: e.tensor_scalar(lbc[:, 0, :], lbc[:, 7, :], -1.0, 1.0, ALU.mult, ALU.add), t)

            (gbank, gt), (bank, t) = linear_pair(["mif", "hq"], yhi, ylo, ytok)
            gts, gfree = TM.get()
            g_tok = A.do(lambda e: e.activation(gts[0:8, 0:S], gbank[0:8, :], ACT.Identity,
                                                bias=pc("mlstm_gate_b", 0, 1, 8)), gt, gfree, t_par)
            PS.put(gbank, g_tok)
            q_toks, fg_tok, fk_tok = [], [], []
            for i in range(4):
                if i:
                    bank, t = linear("hq", yhi, ylo, ytok)
                q_toks.append(A.do(lambda e: e.activation(hq[:, i, :], bank, ACT.Silu), t, ph))
                PS.put(bank, q_toks[i])
            for i in range(4):
                bank, t = linear("hf", yhi, ylo, ytok)
                t = A.do(lambda e: e.activation(hf[:, i, :], bank, ACT.Sigmoid), t, ph)
                PS.put(bank, t)
                fg_tok.append(V.do(lambda e: e.tensor_scalar(hf[:, i, :], hf[:, i, :], lbc[:, 0, i:i + 1],
                                                             lbc[:, 7, i:i + 1], ALU.mult, ALU.add), t, lb_tok))
                fk_tok.append(V.do(lambda e: e.tensor_scalar(hk[:, i, :], hf[:, i, :], -1.0, 1.0,
                                                             ALU.mult, ALU.add), fg_tok[i], ph))
            hv_tok = [None] * 4

            def keep_hv(j, bank, t):
                hv_tok[j] = A.do(lambda e: e.activation(vals[:, j, :], bank, ACT.Copy), t, ph)
                PS.put(bank, hv_tok[j])

            linear_tokens("hi", yhi, ylo, ytok, keep_hv)

            qk_tok = [None] * 8

            def unit_qk(i):
                bank, t = linear("mqk", yhi, ylo, ytok)
                cb, free = TM.get()
                z = V.do(lambda e: e.memset(cb[:, 0:3], 0.0), free)
                t = A.do(lambda e: e.activation(cb[:, 3:3 + S], bank, ACT.Copy), t, free)
                PS.put(bank, t)
                w = [pc("mlstm_conv_w", 8 * j + i) for j in range(4)]
                a = mqk[:, i, :]
                t = V.do(lambda e: e.tensor_scalar(a, cb[:, 0:S], w[0], None, ALU.mult), t, z, ph, t_par)
                for j in range(1, 4):
                    t = V.do(lambda e: e.scalar_tensor_tensor(a, cb[:, j:j + S], w[j], a, ALU.mult, ALU.add), t)
                TM.put(cb, t)
                qk_tok[i] = A.do(lambda e: e.activation(a, a, ACT.Silu, bias=pc("mlstm_conv_b", i)), t)

            gate = {}

            def gates():
                bank, free = PS.get()
                mm = T.do(lambda e: e.matmul(bank[0:4, :], cst[0:8, SEL_C:SEL_C + 4], gts[0:8, 0:S],
                                             start=True, stop=True), g_tok, free, t_cst)
                lf, lfree = TM.get()
                w1, w1free = TM.get()
                t = A.do(lambda e: e.activation(w1[0:4, 0:S], bank[0:4, :], ACT.Abs), mm, w1free)
                t = A.do(lambda e: e.activation(w1[0:4, 0:S], w1[0:4, 0:S], ACT.Exp, scale=-1.0), t)
                t = A.do(lambda e: e.activation(w1[0:4, 0:S], w1[0:4, 0:S], ACT.Ln, bias=1.0), t)
                t = V.do(lambda e: e.scalar_tensor_tensor(lf[0:4, 0:S], bank[0:4, :], 0.0, w1[0:4, 0:S],
                                                          ALU.min, ALU.subtract), t, lfree)
                PS.put(bank, t)
                z = V.do(lambda e: e.memset(w1[0:4, 0:S], 1.0), t)
                bsum, bfree = TM.get()
                t = V.do(lambda e: e.tensor_tensor_scan(bsum[0:4, 0:S], w1[0:4, 0:S], lf[0:4, 0:S], 0.0,
                                                        ALU.mult, ALU.add), t, z, bfree)
                u_tok = V.do(lambda e: e.tensor_tensor(gts[0:4, 0:S], gts[0:4, 0:S], bsum[0:4, 0:S],
                                                       ALU.subtract), t, mm)
                m_tok = V.do(lambda e: e.tensor_tensor_scan(lf[0:4, 0:S], w1[0:4, 0:S], gts[0:4, 0:S], -BIG,
                                                            ALU.mult, ALU.max), u_tok)
                mt_tok = V.do(lambda e: e.tensor_tensor(bsum[0:4, 0:S], bsum[0:4, 0:S], lf[0:4, 0:S], ALU.add), m_tok)
                TM.put(w1, m_tok)
                gate.update(lf=lf, m_tok=m_tok, bsum=bsum, u_tok=u_tok, mt_tok=mt_tok)

            def gate_columns():
                bsum = gate["bsum"]
                bank, free = PS.get()
                T.wait(gate["u_tok"], gate["mt_tok"], free)
                for j in range(4):
                    T.quiet(lambda e: e.matmul(bank[:, 4 * j:4 * j + 4], gts[0:4, 128 * j:128 * j + 128],
                                               cst[0:4, IDENT:IDENT + 4], start=True, stop=True), t_cst)
                for j in range(4):
                    mm = (T.do if j == 3 else T.quiet)(
                        lambda e: e.matmul(bank[0:16, 128:256], cst[0:4, SEL_M + 16 * j:SEL_M + 16 * j + 16],
                                           bsum[0:4, 128 * j:128 * j + 128], start=j == 0, stop=j == 3))
                uc = stat[:, 0:16]
                em, free = TM.get()
                uc_tok = V.do(lambda e: e.tensor_copy(uc, bank[:, 0:16]), mm)
                em_tok = A.do(lambda e: e.activation(em[0:16, 0:128], bank[0:16, 128:256], ACT.Exp, scale=-1.0),
                              mm, uc_tok, free)
                PS.put(bank, em_tok)
                TM.put(gts, mm)
                TM.put(bsum, mm)
                gate.update(uc=uc, em=em, uc_tok=uc_tok, em_tok=em_tok)

            todo = deque([lambda i=i: unit_qk(i) for i in (0, 4, 1, 5, 2, 6, 3, 7)])
            todo.insert(0, gates)
            todo.insert(9, gate_columns)

            def bg():
                if todo:
                    todo.popleft()()

            ad, ao = decay_attention(hq, hk, hf, attd, atto, q_toks, fk_tok, fg_tok, ph, bg)
            while todo:
                bg()
            hbank, hfree = PS.get()
            ho_tok = []
            squares = deque()

            def hgrn_columns(h):
                nonlocal hmm
                buf, t = squares.popleft()
                hmm = add_rows(hbank, 4 * h, buf, h == 0, h == 3, t, hfree)
                TM.put(buf, hmm)

            hmm = None
            for h in range(4):
                bank, t = mix_values(h, vals, 128 * h, attd, atto, [hv_tok, ad[h], ao[h]])
                ho_tok.append(A.do(lambda e: e.activation(hq[:, h, :], bank, ACT.Copy), t))
                PS.put(bank, ho_tok[-1])
                squares.append(square(hq[:, h, :], ho_tok[-1]))
                if h:
                    hgrn_columns(h - 1)
            att_end = [t for t in (T.last(), V.last(), G.last()) if t]

            v_tok = [None] * 4

            def keep_v(j, bank, t):
                v_tok[j] = A.do(lambda e: e.activation(vals[:, j, :], bank, ACT.Copy), t, att_end)
                PS.put(bank, v_tok[j])

            gate_tok = [None] * 8

            def unit_gate(i):
                bank, t = linear("mo" if i < 4 else "hg", yhi, ylo, ytok)
                dst = mo[:, i, :] if i < 4 else hg[:, i - 4, :]
                g = pc("mlstm_norm_g", i) if i < 4 else pc("hgrn_norm_g", i - 4)
                t = A.do(lambda e: e.activation(dst, bank, ACT.Sigmoid if i < 4 else ACT.Silu), t, att_end)
                PS.put(bank, t)
                gate_tok[i] = V.do(lambda e: e.tensor_scalar(dst, dst, g, None, ALU.mult), t, t_par)
                if i >= 4:
                    h = i - 4
                    gate_tok[i] = G.do(lambda e: e.tensor_tensor(hq[:, h, :], hq[:, h, :], dst, ALU.mult),
                                       gate_tok[i], ho_tok[h], hmm)

            todo = deque([lambda i=i: unit_gate(i) for i in (4, 5, 6, 7, 0, 1, 2, 3)])
            starts = [0, 512, 896, 1152]
            attd2 = attd[:, :, :, :].rearrange("p h j t -> p (h j t)")
            atto2 = atto[:, :, :].rearrange("p h t -> p (h t)")
            hk2 = hk[:, :, :].rearrange("p h t -> p (h t)")
            Ws = [attd2[:, 0:1280], atto2[:, 1280:2560]]
            Xs = [atto2[:, 0:1280], hk2[:, 0:1280]]
            w_read, x_read = [att_end, att_end], [att_end, att_end]
            den, dfree = PS.get()
            mbank, mfree = PS.get()
            xt, n_tok = {}, []
            lf, m_tok, uc, em, uc_tok, em_tok = (gate[k] for k in ("lf", "m_tok", "uc", "em", "uc_tok", "em_tok"))

            maxima = {}

            def weights(h):
                W = Ws[h % 2]
                bank, free = PS.get()
                mm = T.do(lambda e: e.matmul(bank, cst[0:4, IDENT + h:IDENT + h + 1].to_broadcast([4, 128]),
                                             lf[0:4, 0:S], start=True, stop=True), m_tok, free)
                dm, dmfree = TM.get()
                t = V.do(lambda e: e.tensor_tensor(dm[:, 0:S].rearrange("p (j t) -> p j t", j=4),
                                                   bank.rearrange("p (j t) -> p j t", j=4),
                                                   bc(cst[:, CAUS:CAUS + 128], 4, 1), ALU.add), mm, dmfree)
                wt = []
                for j in range(4):
                    a, bias = starts[j], uc[:, 4 * j + h:4 * j + h + 1]
                    Wj = W[:, a:a + 512 - 128 * j]
                    wt.append(A.do(lambda e: e.activation(
                        Wj[:, 0:128], dm[:, 128 * j:128 * j + 128], ACT.Exp, bias=bias, scale=-1.0),
                        t, uc_tok, w_read[h % 2]))
                    if j < 3:
                        wt[-1] = A.do(lambda e: e.activation(
                            Wj[:, 128:512 - 128 * j], bank[:, 128 * j + 128:512], ACT.Exp, bias=bias, scale=-1.0), mm)
                PS.put(bank, wt[-1])
                TM.put(dm, wt[-1])
                maxima[h] = wt

            def scored(h):
                W, X, wt = Ws[h % 2], Xs[h % 2], maxima[h]
                xt[h] = []
                for j in range(4):
                    a, wd = starts[j], 512 - 128 * j
                    sbank, free = PS.get()
                    mm = T.do(lambda e: e.matmul(
                        sbank[:, 0:wd], mqk[:, 4 + h, 128 * j:128 * j + 128], mqk[:, h, 128 * j:512],
                        start=True, stop=True), qk_tok[h], qk_tok[4 + h], free)
                    xt[h].append(V.do(lambda e: e.scalar_tensor_tensor(
                        X[:, a:a + wd], sbank[:, 0:wd], 128.0 ** -0.5, W[:, a:a + wd], ALU.mult, ALU.mult),
                        mm, wt[j], x_read[h % 2]))
                    PS.put(sbank, xt[h][-1])
                w_read[h % 2] = xt[h][-1]

            def outputs(h):
                X = Xs[h % 2]
                bank, free = PS.get()
                T.wait(free, v_tok, xt[h], dfree)
                for j in range(4):
                    a, wd = starts[j], 512 - 128 * j
                    T.quiet(lambda e: e.matmul(
                        bank[:, 128 * j:512], vals[:, j, 128 * h:128 * h + 128], X[:, a:a + wd],
                        start=j == 0, stop=j == 3))
                for j in range(4):
                    for i in range(j, 4):
                        a = starts[j] + 128 * (i - j)
                        mm = (T.do if (i, j) == (3, 3) else T.quiet)(
                            lambda e: e.matmul(den[0:16, 0:128], to_row(4 * h + i), X[:, a:a + 128],
                                               start=(h, i, j) == (0, 0, 0), stop=(h, i, j) == (3, 3, 3)))
                x_read[h % 2] = mm
                n_tok.append(A.do(lambda e: e.activation(mqk[:, h, :], bank, ACT.Copy), mm))
                PS.put(bank, n_tok[-1])
                squares.append(square(mqk[:, h, :], n_tok[-1]))
                return mm

            def norm_columns(h):
                buf, t = squares.popleft()
                m2 = add_rows(mbank, 4 * h, buf, h == 0, h == 3, t, mfree)
                TM.put(buf, m2)
                return m2

            def hgrn_norm():
                mod_column(5)
                for h in range(4):
                    R, t = spread(rows, 4 * h)
                    gate_tok[4 + h] = V.do(lambda e: e.tensor_tensor(hq[:, h, :], hq[:, h, :], R, ALU.mult),
                                           t, gate_tok[4 + h])
                    PS.put(R, gate_tok[4 + h])
                TM.put(rows[0], t)

            def some(n):
                for _ in range(min(n, len(todo))):
                    todo.popleft()()

            weights(0)
            weights(1)
            hgrn_columns(3)
            linear_tokens("mv", yhi, ylo, ytok, keep_v)
            scored(0)
            weights(2)
            some(1)
            scored(1)
            weights(3)
            rows = root(hbank, hmm, 1 / 128)
            some(1)
            outputs(0)
            some(1)
            norm_columns(0)
            scored(2)
            outputs(1)
            some(1)
            norm_columns(1)
            scored(3)
            some(1)
            outputs(2)
            hgrn_norm()
            some(1)
            norm_columns(2)
            mm = outputs(3)
            some(1)
            m2 = norm_columns(3)
            some(1)
            y_read = T.last()
            x_tok = [None] * 8
            x_tok[4:8] = to_y([(4 + h, hq[:, h, :], gate_tok[4 + h]) for h in range(4)], y_read)
            for h in range(4):
                gate_tok[h] = G.do(lambda e: e.tensor_tensor(mo[:, h, :], mo[:, h, :], mqk[:, h, :], ALU.mult),
                                   gate_tok[h], n_tok[h], m2)
            TM.put(lf, T.last())
            d, dfree = TM.get()
            dv = d[0:16, 0:128]
            t = A.do(lambda e: e.activation(dv, den[0:16, 0:128], ACT.Abs), mm, dfree)
            PS.put(den, t)
            t = V.do(lambda e: e.tensor_tensor(dv, dv, em[0:16, 0:128], ALU.max), t, em_tok)
            TM.put(em, t)
            t = V.do(lambda e: e.tensor_scalar(dv, dv, 1e18, None, ALU.min), t)
            t = V.do(lambda e: e.scalar_tensor_tensor(dv, dv, EPS, dv, ALU.mult, ALU.mult), t)
            t = V.do(lambda e: e.scalar_tensor_tensor(dv, mbank[0:16, 0:128], 1 / 128, dv, ALU.mult, ALU.add), m2, t)
            PS.put(mbank, t)
            t = A.do(lambda e: e.activation(dv, dv, ACT.Sqrt), t)
            d_tok = V.do(lambda e: e.reciprocal(dv, dv), t)
            tiles, toks = [], []
            sums = Sums()
            order = [4, 5, 6, 7, 0, 1, 2, 3]

            def mlstm_normed():
                mod_column(7)
                spreads = [spread((d, d_tok), 4 * h) for h in range(4)]
                TM.put(d, spreads[-1][1])
                items = []
                for h, (R, t) in enumerate(spreads):
                    t = V.do(lambda e: e.tensor_tensor(mo[:, h, :], mo[:, h, :], R, ALU.mult), t, gate_tok[h])
                    PS.put(R, t)
                    items.append((h, mo[:, h, :], t))
                x_tok[0:4] = to_y(items, y_read)

            first = deque(linear_pair(["wout", "wout"], yhi, ylo, x_tok, order, {0: mlstm_normed}))
            for n in range(NT):
                bank, t = first.popleft() if first else linear("wout", yhi, ylo, x_tok, order)
                if n == 0:
                    need_mods(5, 7, 6)
                dst = attd[:, n, :, :].rearrange("p j t -> p (j t)") if n < 4 else hk[:, n - 4, :]
                t = A.do(lambda e: e.activation(dst, bank, ACT.Copy), t, x_read[0], x_read[1], w_read[0], w_read[1])
                PS.put(bank, t)
                sums.add(dst, t, n == NT - 1)
                tiles.append(dst)
                toks.append(t)
            y_free[0] = T.last()
            sums = postnorm(tiles, toks, sums, pc("mix_post_g", 0, 8), 5, 1.0)
        phase_end()

        ytok = prenorm(pc("ffn2_pre_g", 0, 8), 6, 7, sums)
        sums = gated_ffn("ffn2", ytok, pc("ffn2_post_g", 0, 8), 8, 10, 9)

        ytok = prenorm(pc("norm_g_2", 0, 8), 9, 10, sums)
        with ExitStack() as st:
            ph = state["phase"]
            qk = sb("gqk", [128, 8, S], fp32, st)
            q, k = qk[:, 0:4, :], qk[:, 4:8, :]
            fd = sb("gf", [128, 4, S], fp32, st)
            vals = sb("gvals", [128, 4, D], fp32, st)
            rg = sb("grg", [128, 8, S], fp32, st)
            attd = sb("gattd", [128, 4, 4, 128], fp32, st)
            atto = sb("gatto", [128, 4, 768], fp32, st)

            ga2, free2 = TM.get()
            s_a2 = sem("s_a2")
            t_a2 = Y.dma(lambda e: e.dma_start(ga2[0:16, 0:S], dram["a2"]), (s_a2, 16), free2)
            (abank, at), (bank, t) = linear_pair(["ga", "gq"], yhi, ylo, ytok)
            alr, free = TM.get()
            t_a = A.do(lambda e: e.activation(alr[0:16, 0:S], abank[0:16, :], ACT.Copy), at, free)
            PS.put(abank, t_a)
            qt, kt_, ft = [], [], []
            for i in range(4):
                if i:
                    bank, t = linear("gq", yhi, ylo, ytok)
                qt.append(A.do(lambda e: e.activation(q[:, i, :], bank, ACT.Copy, scale=128.0 ** -0.5), t, ph))
                PS.put(bank, qt[-1])
            for i in range(4):
                bank, free = PS.get()
                mm = T.do(lambda e: e.matmul(bank, ga2[0:16, 128 * i:128 * i + 128], alr[0:16, 0:S],
                                             start=True, stop=True), t_a, t_a2, free)
                z, zfree = TM.get()
                l, lfree = TM.get()
                t = A.do(lambda e: e.activation(z[:, 0:S], bank, ACT.Identity, bias=pc("gla_b_a_2", i)), mm, zfree)
                PS.put(bank, t)
                t1 = A.do(lambda e: e.activation(l[:, 0:S], z[:, 0:S], ACT.Abs), t, lfree)
                t1 = A.do(lambda e: e.activation(l[:, 0:S], l[:, 0:S], ACT.Exp, scale=-1.0), t1)
                t1 = A.do(lambda e: e.activation(l[:, 0:S], l[:, 0:S], ACT.Ln, bias=1.0), t1)
                t1 = V.do(lambda e: e.scalar_tensor_tensor(z[:, 0:S], z[:, 0:S], 0.0, l[:, 0:S],
                                                           ALU.min, ALU.subtract), t1)
                ft.append(A.do(lambda e: e.activation(fd[:, i, :], z[:, 0:S], ACT.Exp, scale=1 / 16), t1, ph))
                TM.put(z, ft[-1])
                TM.put(l, t1)
                bank, t = linear("gk", yhi, ylo, ytok)
                kt_.append(A.do(lambda e: e.activation(k[:, i, :], bank, ACT.Copy), t, ph))
                PS.put(bank, kt_[-1])
            TM.put(alr, mm)
            TM.put(ga2, mm)
            v_tok = []
            for half in range(2):
                def keep_v(j, bank, t):
                    v_tok.append(A.do(lambda e: e.activation(vals[:, j, 512 * half:512 * half + 512], bank, ACT.Copy),
                                      t, ph))
                    PS.put(bank, v_tok[-1])
                linear_tokens("gv", yhi, ylo, ytok, keep_v)
            r_toks = [None] * 8

            def unit_r(i):
                bank, t = linear("gr", yhi, ylo, ytok)
                t = A.do(lambda e: e.activation(rg[:, i, :], bank, ACT.Silu, bias=pc("gla_b_r_2", i)), t, ph, t_par)
                PS.put(bank, t)
                r_toks[i] = V.do(lambda e: e.tensor_scalar(rg[:, i, :], rg[:, i, :], pc("gla_norm_g_2", i % 2), None,
                                                           ALU.mult), t)

            todo2 = deque([lambda i=i: unit_r(i) for i in range(8)])

            def bg2():
                if todo2:
                    todo2.popleft()()

            ad, ao = decay_attention(q, k, fd, attd, atto, qt, kt_, ft, ph, bg2)
            while todo2:
                bg2()
            y_read = T.last()
            g_tok = []
            x_tok = [None] * 8
            got = [PS.get() for _ in range(2)]
            squares, rows2, mms = deque(), [None] * 2, {}

            def value_columns(i):
                buf, t = squares.popleft()
                sbank, sfree = got[i // 4]
                mms[i] = add_rows(sbank, 4 * (i // 2), buf, i % 4 == 0, i % 4 == 3, t, sfree)
                TM.put(buf, mms[i])
                if i % 4 == 3:
                    rows2[i // 4] = root(sbank, mms[i], 1.0 / 256)

            def heads_normed(half):
                mod_column((11, 13)[half])
                hs = (2 * half, 2 * half + 1)
                spreads = [spread(rows2[half], 4 * h) for h in hs]
                TM.put(rows2[half][0], spreads[-1][1])
                items = []
                for h, (R, t_r) in zip(hs, spreads):
                    for i in (2 * h, 2 * h + 1):
                        t = V.do(lambda e: e.tensor_tensor(rg[:, i, :], rg[:, i, :], R, ALU.mult), t_r, g_tok[i])
                        if i % 2:
                            PS.put(R, t)
                        items.append((i, rg[:, i, :], t))
                x_tok[4 * half:4 * half + 4] = to_y(items, y_read)

            for i in range(8):
                bank, t = mix_values(i // 2, vals, 128 * i, attd, atto, [v_tok, ad[i // 2], ao[i // 2]])
                buf, free = TM.get()
                t1 = A.do(lambda e: e.activation(buf[:, 0:S], bank, ACT.Square), t, free)
                g_tok.append(V.do(lambda e: e.tensor_tensor(rg[:, i, :], rg[:, i, :], bank, ALU.mult), t1, r_toks[i]))
                PS.put(bank, g_tok[-1])
                squares.append((buf, t1))
                if i:
                    value_columns(i - 1)
                if i == 2:
                    ready_root()
                if i == 5:
                    heads_normed(0)
            value_columns(7)
            result, sums = add_gated(11, 0, 13, 12)
            first = deque(linear_pair(["go", "go"], yhi, ylo, x_tok, None, {4: lambda: heads_normed(1)}))
            for n in range(NT):
                bank, t = first.popleft() if first else linear("go", yhi, ylo, x_tok)
                PS.put(bank, result(0, n, bank, t))
            y_free[0] = T.last()
        phase_end()

        ytok = prenorm(pc("norm_g_2", 8, 8), 12, 13, sums)
        result, sums = add_gated(14, 3, 16, 15)
        ffn("mlp0", ytok, [8] * 4, False, result)
        phase_end()

        ytok = prenorm(pc("norm_g_2", 16, 8), 15, 16, sums)
        with ExitStack() as st:
            ph = state["phase"]
            qs = sb("dq", [128, 8, S], fp32, st)
            ks = sb("dk", [128, 8, S], fp32, st)
            vals = sb("dvals", [128, 4, D], fp32, st)
            cosr = sb("cosr", [128, S], fp32, st)
            sinr = sb("sinr", [128, S], fp32, st)
            pp = sb("dp", [128, 5, 2, S], fp32, st)
            aT = sb("daT", [128, 2, S], fp32, st)
            sm = sb("dsm", [128, 5, 8], fp32, st)
            s_pos = sem("s_pos")
            kf, kff = TM.get()
            posi = kf[:, 0:S].bitcast(i32)
            t_pos = Y.dma(lambda e: e.dma_start(posi, dram["pos"]), (s_pos, 16), kff)
            heads = deque(linear_pair(["dqk", "dqk"], yhi, ylo, ytok))

            def copied(bank, t):
                x, xf = TM.get()
                t = A.do(lambda e: e.activation(x[:, 0:S], bank, ACT.Copy), t, xf)
                PS.put(bank, t)
                return x, t

            def turned_pair(x, t):
                bank, free = PS.get()
                mm = T.do(lambda e: e.matmul(bank, cst[:, PERM:PERM + 128], x[:, 0:S], start=True, stop=True), t, free)
                return x, bank, mm

            def rotated(dst, x, bank, mm):
                a = V.do(lambda e: e.tensor_tensor(dst, bank, sinr[:, :], ALU.mult), mm, s_tok, ph)
                PS.put(bank, a)
                b = G.do(lambda e: e.tensor_tensor(x[:, 0:S], x[:, 0:S], cosr[:, :], ALU.mult), mm, c_tok)
                t = G.do(lambda e: e.tensor_tensor(dst, dst, x[:, 0:S], ALU.add), a, b)
                TM.put(x, t)
                return t

            pairs = [copied(*head) for head in heads]
            pairs.append(copied(*linear("dqk", yhi, ylo, ytok)))

            ang, af = TM.get()
            t = V.do(lambda e: e.tensor_copy(ang[:, 0:S], posi), t_pos, af)
            t = V.do(lambda e: e.tensor_scalar(ang[:, 0:S], ang[:, 0:S], cst[:, INVF_C:INVF_C + 1], None, ALU.mult), t)
            t = V.do(lambda e: e.tensor_scalar(kf[:, 0:S], ang[:, 0:S], 1 / (2 * math.pi), MAGIC, ALU.mult, ALU.add),
                     t)
            t = V.do(lambda e: e.tensor_scalar(kf[:, 0:S], kf[:, 0:S], MAGIC, None, ALU.subtract), t)
            for part in (PI_A, PI_B, PI_C):
                t = V.do(lambda e: e.scalar_tensor_tensor(ang[:, 0:S], kf[:, 0:S], -part, ang[:, 0:S],
                                                          ALU.mult, ALU.add), t)
            t = V.do(lambda e: e.tensor_scalar(ang[:, 0:S], ang[:, 0:S], -3.1415925, 3.1415925, ALU.max, ALU.min), t)
            s_tok = A.do(lambda e: e.activation(sinr[:, :], ang[:, 0:S], ACT.Sin), t, ph)
            t = A.do(lambda e: e.activation(kf[:, 0:S], ang[:, 0:S], ACT.Abs), t)
            c_tok = A.do(lambda e: e.activation(cosr[:, :], kf[:, 0:S], ACT.Sin, bias=cst[:, HPI_C:HPI_C + 1],
                                                scale=-1.0), t, ph)
            TM.put(ang, s_tok, t)
            TM.put(kf, c_tok)
            L = [pc("diff_lambda_2", 64 * i, 64) for i in range(4)]
            for i in range(2):
                buf, free = TM.get()
                t = V.do(lambda e: e.tensor_tensor(buf[:, 0:64], L[2 * i], L[2 * i + 1], ALU.mult), free, t_par)
                t = V.do(lambda e: e.tensor_reduce(lamb[:, i:i + 1], buf[:, 0:64], AX.X, ALU.add), t)
                TM.put(buf, t)
            t = A.do(lambda e: e.activation(lamb[:, 2:4], lamb[:, 0:2], ACT.Exp), t)
            t = V.do(lambda e: e.tensor_tensor(lamb[:, 4:5], lamb[:, 3:4], lamb[:, 2:3], ALU.subtract), t)
            t = V.do(lambda e: e.tensor_scalar(lamb[:, 4:5], lamb[:, 4:5], LAMBDA_INIT, None, ALU.subtract), t)
            lam_tok = V.do(lambda e: e.tensor_scalar(lamb[:, 5:6], pc("diff_subln_g_2"), 1.0 - LAMBDA_INIT, None,
                                                     ALU.mult), t)

            v_tok = []
            for half in range(2):
                def keep_dv(j, bank, t):
                    v_tok.append(A.do(lambda e: e.activation(vals[:, j, 512 * half:512 * half + 512], bank, ACT.Copy),
                                      t, ph))
                    PS.put(bank, v_tok[-1])
                linear_tokens("dv", yhi, ylo, ytok, keep_dv)
                if half == 0:
                    pairs = [rotated(dst, *turned_pair(*x))
                             for dst, x in zip((qs[:, 0, :], ks[:, 0, :], qs[:, 1, :]), pairs)]
                    qk_toks = {0: pairs[:2], 1: pairs[2:]}

            p_free, a_free = [None] * 5, [None] * 2
            o_tok = []

            def softmaxes(n, h, i):
                wd = 128 * (i + 1)
                got = [PS.get() for _ in range(2)]
                m, p = sm[:, n, :], pp[:, n, :, :]
                mms = []
                for c in range(2):
                    bank, free = got[c]
                    rows = slice(64 * c, 64 * c + 64)
                    mms.append(T.do(lambda e: e.matmul(
                        bank[:, 0:wd], qs[rows, h, 128 * i:128 * i + 128], ks[rows, h, 0:wd], start=True, stop=True),
                        qk_toks[h], free))
                mx = []
                for c in range(2):
                    bank = got[c][0]
                    d = bank[:, 128 * i:wd]
                    t = V.do(lambda e: e.tensor_tensor(d, d, cst[:, CNEG:CNEG + 128], ALU.add), mms[c])
                    t = V.do(lambda e: e.tensor_reduce(m[:, c:c + 1], bank[:, 0:wd], AX.X, ALU.max), t, p_free[n])
                    mx.append(t)
                t = V.do(lambda e: e.tensor_scalar(m[:, 2:4], m[:, 0:2], -0.125, None, ALU.mult), mx)
                ex = []
                for c in range(2):
                    bank = got[c][0]
                    ex.append(A.do(lambda e: e.activation(
                        p[:, c, 0:wd], bank[:, 0:wd], ACT.Exp, bias=m[:, 2 + c:3 + c], scale=0.125,
                        accum_out=m[:, 4 + c:5 + c]), t, ph, p_free[n]))
                    PS.put(bank, ex[-1])
                return ex

            def combined(n, h, i, ex):
                wd = 128 * (i + 1)
                m, p = sm[:, n, :], pp[:, n, :, :]
                t = V.do(lambda e: e.reciprocal(m[:, 6:8], m[:, 4:6]), ex)
                t = V.do(lambda e: e.tensor_tensor(m[:, 7:8], m[:, 7:8], lamb[:, 4:5], ALU.mult), t, lam_tok)
                t1 = V.do(lambda e: e.tensor_scalar(p[:, 1, 0:wd], p[:, 1, 0:wd], m[:, 7:8], None, ALU.mult), t)
                return V.do(lambda e: e.scalar_tensor_tensor(p[:, 0, 0:wd], p[:, 0, 0:wd], m[:, 6:7],
                                                             p[:, 1, 0:wd], ALU.mult, ALU.add), t1)

            def turned(s, h, i, tok):
                n, wd = s % 5, 128 * (i + 1)
                bank, free = PS.get()
                T.wait(free, tok)
                for j in range(i + 1):
                    c = slice(128 * j, 128 * j + 128)
                    mm = (T.do if j == i else T.quiet)(lambda e: e.transpose(bank[:, c], pp[:, n, 0, c], ident))
                p_free[n] = mm
                t = A.do(lambda e: e.activation(aT[:, s % 2, 0:wd], bank[:, 0:wd], ACT.Copy), mm, a_free[s % 2], ph)
                PS.put(bank, t)
                return t

            obanks = {}

            def values(s, h, i, tok):
                if i == 0:
                    obanks[h] = PS.get()
                obank, ofree = obanks[h]
                for j in range(i + 1):
                    mm = (T.do if j == i else T.quiet)(lambda e: e.matmul(
                        obank[:, 128 * i:128 * i + 128], vals[:, j, 128 * h:128 * h + 128],
                        aT[:, s % 2, 128 * j:128 * j + 128], start=j == 0, stop=j == i), tok, v_tok, ofree)
                a_free[s % 2] = mm
                if i < 3:
                    return
                t = A.do(lambda e: e.activation(qs[:, h, :], obank, ACT.Copy), mm)
                o_tok.append(t)
                PS.put(obank, t)
                squares.append((h, *square(qs[:, h, :], t)))

            squares, nbanks, rows2 = deque(), {}, {}
            groups = (0, 0, 0, 0, 1, 1, 1, 2)

            def norm_columns():
                h, buf, t = squares.popleft()
                g = groups[h]
                if g not in nbanks:
                    nbanks[g] = PS.get()
                bank, free = nbanks[g]
                end = h in (3, 6, 7)
                mm = add_rows(bank, 4 * (h - 4 * g + g // 2), buf, h in (0, 4, 7), end, t, free)
                TM.put(buf, mm)
                if end:
                    rows2[g] = root(bank, mm, 1 / 128)

            def normed(h):
                g = groups[h]
                R, t = spread(rows2[g], 4 * (h - 4 * g + g // 2))
                if h in (3, 6, 7):
                    TM.put(rows2[g][0], t)
                t = V.do(lambda e: e.scalar_tensor_tensor(qs[:, h, :], qs[:, h, :], lamb[:, 5:6], R,
                                                          ALU.mult, ALU.mult), t, o_tok[h], lam_tok)
                PS.put(R, t)
                return t

            x_tok = [None] * 8
            steps = [(h, i) for h in range(8) for i in range(4)]
            exs, cs, ts, n_toks, came = {}, {}, {}, {}, []
            for s in range(len(steps) + 4):
                if s < 32:
                    h, i = steps[s]
                    exs[s] = softmaxes(s % 5, h, i)
                if 0 <= s - 3 < 32:
                    ts[s - 3] = turned(s - 3, *steps[s - 3], cs[s - 3])
                if came:
                    (hh, dst), x = came.pop()
                    qk_toks.setdefault(hh, []).append(rotated(dst[:, hh, :], *turned_pair(*x)))
                if s < 26 and i % 2 == 0:
                    parts = linear_halves("dqk", yhi, ylo, ytok)
                    next(parts)
                elif s < 26:
                    came.append(((h + 1, ks) if i == 1 else (h + 2, qs), copied(*next(parts))))
                    y_read = T.last()
                if 0 <= s - 1 < 32:
                    cs[s - 1] = combined((s - 1) % 5, *steps[s - 1], exs[s - 1])
                while squares:
                    norm_columns()
                if 0 <= s - 4 < 32:
                    values(s - 4, *steps[s - 4], ts[s - 4])
                if 21 <= s < 25:
                    n_toks[s - 21] = normed(s - 21)
                if 28 <= s < 32:
                    x_tok[s - 28:s - 27] = to_y([(s - 28, qs[:, s - 28, :], n_toks[s - 28])], y_read)
                if s == 33:
                    x_tok[4:7] = to_y([(h, qs[:, h, :], normed(h)) for h in (4, 5, 6)], y_read)

            def last_normed():
                norm_columns()
                x_tok[7:8] = to_y([(7, qs[:, 7, :], normed(7))], y_read)

            result, sums = add_gated(17, 0, 19, 18)
            first = deque(linear_pair(["do", "do"], yhi, ylo, x_tok, None, {7: last_normed}))
            for n in range(NT):
                bank, t = first.popleft() if first else linear("do", yhi, ylo, x_tok)
                PS.put(bank, result(0, n, bank, t))
            y_free[0] = T.last()
        phase_end()

        ytok = prenorm(pc("norm_g_2", 24, 8), 18, 19, sums)
        result, sums = add_gated(20, 3)
        ffn("mlp1", ytok, [8] * 4, False, result)

        R, r_tok = sums.root(None)
        for n in range(NT):
            buf, free = TM.get()
            t = V.do(lambda e: e.scalar_tensor_tensor(
                buf[:, 0:S], h_sb[:, n, :], pc("final_g_2", n), R, ALU.mult, ALU.mult), r_tok, free, htok[n])
            Y.dma(lambda e: e.dma_start(out[n], buf[:, 0:S]), (s_out[n], 16), t)
            TM.put(buf, (s_out[n], 16))
        assert state["at"] == len(stream) and not state["prepped"]
        block = ctx.enter_context(nc.Block())

        @block.sync
        def _(e):
            for n in range(NT):
                e.wait_ge(s_out[n], 16)


def by_feature(w):
    k, n = w.shape
    return w.reshape(k // 128, 128, n // 128, 128).transpose(2, 1, 0, 3).reshape(n // 128, 128, k)


def by_rows(w):
    n = w.shape[1] // 512
    return w.reshape(4, 2, 128, n, 512).transpose(3, 0, 2, 1, 4).reshape(4 * n, 128, 1024)


def lay_out(x):
    d = {}
    offs, n_par = param_offsets()
    par = np.zeros((128, n_par), np.float32)
    for name, n in PARAMS:
        a = x[name].reshape(-1)
        if name == "mlstm_gate_b":
            par[0:8, offs[name]] = a
        elif name == "diff_lambda_2":
            par[:, offs[name]:offs[name] + n] = a[None, :]
        else:
            par[:, offs[name]:offs[name] + n] = a.reshape(n, 128).T
    d["par"] = par
    d["cst"], d["msk"] = constants()
    d["x"] = x["x"][0].T.reshape(8, 128, S).transpose(1, 0, 2)
    d["pos"] = np.broadcast_to(x["positions_2"].reshape(1, S), (128, S))
    d["a2"] = x["gla_w_a2_2"][0]
    d["ada"] = x["ada_w"][0].reshape(8, 128, 9, 1024).transpose(2, 0, 1, 3)
    d["ada_2"] = x["ada_w_2"].reshape(2, 8, 128, 6, 1024).transpose(0, 3, 1, 2, 4).reshape(12, 8, 128, 1024)
    for b in ("ffn1", "ffn2"):
        gate, up, down = (x[f"{b}_w_{p}"][0] for p in ("gate", "up", "down"))
        for g in range(3):
            c = slice(128 * sum(FFN_GROUPS[:g]), 128 * sum(FFN_GROUPS[:g + 1]))
            a, u = by_feature(gate[:, c]), by_feature(up[:, c])
            d[f"{b}_up{g}"] = np.stack([a, u], 1).reshape(-1, 128, 1024)
            d[f"{b}_dn{g}"] = by_feature(down[c])
    w = x["w_in"][0]
    d["w_mqk"] = by_feature(w[:, 0:1024])
    d["w_mif"] = by_feature(w[:, 2048:2176])
    d["w_mv"] = by_rows(w[:, 1024:1536])
    d["w_mo"] = by_feature(w[:, 1536:2048])
    d["w_hq"] = by_feature(w[:, 2056:2568])
    d["w_hf"] = by_feature(w[:, 2568:3080])
    d["w_hi"] = by_rows(w[:, 3080:3592])
    d["w_hg"] = by_feature(w[:, 3592:4104])
    d["w_wout"] = by_feature(x["w_out"][0])
    w = x["gla_w_in_2"][0]
    d["w_gq"] = by_feature(w[:, 0:512])
    d["w_gk"] = by_feature(w[:, 512:1024])
    d["w_gv"] = by_rows(w[:, 1024:2048])
    d["w_gr"] = by_feature(w[:, 2048:3072])
    d["w_ga"] = by_feature(np.concatenate([w[:, 3072:3088], w[:, 0:112]], 1))
    d["w_go"] = by_feature(x["gla_w_o_2"][0])
    w = x["diff_w_in_2"][0]
    q, k = by_feature(w[:, 0:1024]), by_feature(w[:, 1024:2048])
    d["w_dqk"] = np.stack([q, k], 1).reshape(16, 128, 1024)
    d["w_dv"] = by_rows(w[:, 2048:3072])
    d["w_do"] = by_feature(x["diff_w_o_2"][0])
    for layer in range(2):
        w1, w2 = x["mlp_w1_2"][layer], x["mlp_w2_2"][layer]
        for g in range(4):
            c = slice(1024 * g, 1024 * g + 1024)
            d[f"mlp{layer}_up{g}"] = by_feature(w1[:, c])
            d[f"mlp{layer}_dn{g}"] = by_feature(w2[c])
    return {k: np.ascontiguousarray(v) for k, v in d.items()}


def kernel(**inputs):
    import concourse.bacc as bacc
    from concourse.bass_utils import run_bass_kernel_spmd

    arrays = lay_out({k: np.asarray(v) for k, v in inputs.items()})
    nc = bacc.Bacc("TRN2", target_bir_lowering=False, num_devices=1)
    dram, feed = {}, {}
    for name, a in arrays.items():
        feed[f"in_{name}"] = a
        dram[name] = nc.dram_tensor(f"in_{name}", a.shape, mybir.dt.from_np(a.dtype), kind="ExternalInput").ap()
    out = nc.dram_tensor("out_y", (NT, 128, S), mybir.dt.float32, kind="ExternalOutput").ap()
    build_program(nc, dram, out)
    got = run_bass_kernel_spmd(nc, [feed], core_ids=[0]).results[0]["out_y"]
    return np.ascontiguousarray(np.asarray(got).reshape(D, S).T).reshape(1, S, D)
```
